# Optimizing a Trainium2 kernel written in Bass

```python
import jax, jax.numpy as jnp
from jax import lax
import numpy as np

D_MODEL = 1024
BATCH = 1
SEQ = 1024
DEPTH = 1
DEC_BATCH = 8
DEC_SEQ = 1
PAST_LEN = 2048
PAGE_SIZE = 128

HEAD_DIM = 64
ATTN_WIDTH = D_MODEL // 2
N_HEADS = ATTN_WIDTH // HEAD_DIM
N_KV_HEADS = 2
Q_PER_KV = N_HEADS // N_KV_HEADS
KV_WIDTH = N_KV_HEADS * HEAD_DIM
WINDOW = 128
ROPE_THETA = 10000.0
LRU_WIDTH = D_MODEL - ATTN_WIDTH
LRU_HEADS = 8
LRU_BLOCK = LRU_WIDTH // LRU_HEADS
CONV_WIDTH = 4
LRU_C = 8.0
IN_WIDTH = ATTN_WIDTH + 2 * KV_WIDTH + 2 * LRU_WIDTH
SPLITS = [ATTN_WIDTH, ATTN_WIDTH + KV_WIDTH, ATTN_WIDTH + 2 * KV_WIDTH, ATTN_WIDTH + 2 * KV_WIDTH + LRU_WIDTH]
N_GROUPS = 4
EXPERTS_PER_GROUP = 8
TOP_K = 2
D_EXPERT = D_MODEL // 4
EPS = 1e-6
NEG_INF = -1e30

kernel_name = "hymba_rglru_swa_sink_hmoe_step"

def rmsnorm(x, g):
    xf = x.astype(jnp.float32)
    y = xf * lax.rsqrt(jnp.mean(xf * xf, axis=-1, keepdims=True) + EPS)
    return (y * g.astype(jnp.float32)).astype(x.dtype)

def rotary(x, pos):
    half = HEAD_DIM // 2
    inv = ROPE_THETA ** (-2.0 * jnp.arange(half, dtype=jnp.float32) / HEAD_DIM)
    ang = pos.astype(jnp.float32)[:, None] * inv[None, :]
    cos = jnp.cos(ang)[None, :, None, :]
    sin = jnp.sin(ang)[None, :, None, :]
    xf = x.astype(jnp.float32)
    x1, x2 = xf[..., :half], xf[..., half:]
    return jnp.concatenate([x1 * cos - x2 * sin, x2 * cos + x1 * sin], axis=-1).astype(x.dtype)

def in_proj(x, ln_g, w_in):
    B, T, _ = x.shape
    u = rmsnorm(x, ln_g) @ w_in
    q, k, v, xl, yg = jnp.split(u, SPLITS, axis=-1)
    return (q.reshape(B, T, N_HEADS, HEAD_DIM), k.reshape(B, T, N_KV_HEADS, HEAD_DIM),
            v.reshape(B, T, N_KV_HEADS, HEAD_DIM), xl, yg)

def sink_attention(q, k, v, qpos, kpos, sinks):
    s = jnp.einsum('bnqkgd,bnskd->bnkgqs', q, k).astype(jnp.float32) * (HEAD_DIM ** -0.5)
    dq = qpos[:, :, None] - kpos[:, None, :]
    mask = (kpos[:, None, :] >= 0) & (dq >= 0) & (dq < WINDOW)
    s = jnp.where(mask[None, :, None, None], s, NEG_INF)
    sink = sinks.astype(jnp.float32).reshape(N_KV_HEADS, Q_PER_KV)[None, None, :, :, None, None]
    m = jnp.maximum(jnp.max(s, axis=-1, keepdims=True), sink)
    p = jnp.exp(s - m)
    p = p / (jnp.sum(p, axis=-1, keepdims=True) + jnp.exp(sink - m))
    return jnp.einsum('bnkgqs,bnskd->bnqkgd', p.astype(v.dtype), v)

def swa_prompt(q, k, v, sinks):
    B, T = q.shape[:2]
    n = T // WINDOW
    qb = q.reshape(B, n, WINDOW, N_KV_HEADS, Q_PER_KV, HEAD_DIM)
    kb = k.reshape(B, n, WINDOW, N_KV_HEADS, HEAD_DIM)
    vb = v.reshape(B, n, WINDOW, N_KV_HEADS, HEAD_DIM)
    pad = ((0, 0), (1, 0), (0, 0), (0, 0), (0, 0))
    kc = jnp.concatenate([jnp.pad(kb, pad)[:, :-1], kb], axis=2)
    vc = jnp.concatenate([jnp.pad(vb, pad)[:, :-1], vb], axis=2)
    qpos = jnp.arange(T).reshape(n, WINDOW)
    kpos = jnp.concatenate([qpos - WINDOW, qpos], axis=1)
    out = sink_attention(qb, kc, vc, qpos, kpos, sinks)
    keep = min(WINDOW, T)
    return out.reshape(B, T, ATTN_WIDTH), k[:, T - keep:], v[:, T - keep:]

def swa_sample(q, k, v, cache_k, cache_v, sinks):
    DB, Tq = q.shape[:2]
    buf = cache_k.shape[1]
    kc = jnp.concatenate([cache_k.astype(k.dtype), k], axis=1)
    vc = jnp.concatenate([cache_v.astype(v.dtype), v], axis=1)
    qpos = PAST_LEN + jnp.arange(Tq)
    kpos = jnp.concatenate([PAST_LEN - buf + jnp.arange(buf), qpos])
    out = sink_attention(q.reshape(DB, 1, Tq, N_KV_HEADS, Q_PER_KV, HEAD_DIM),
                         kc[:, None], vc[:, None], qpos[None], kpos[None], sinks)
    keep = min(WINDOW, kc.shape[1])
    return out.reshape(DB, Tq, ATTN_WIDTH), kc[:, kc.shape[1] - keep:], vc[:, vc.shape[1] - keep:]

def rglru(xl, conv_buf, h0, w_conv, b_conv, w_a, b_a, w_x, b_x, lam):
    B, T, _ = xl.shape
    xpad = jnp.concatenate([conv_buf.astype(xl.dtype), xl], axis=1)
    c = b_conv + w_conv[0] * xpad[:, 0:T]
    for j in range(1, CONV_WIDTH):
        c = c + w_conv[j] * xpad[:, j:j + T]
    new_buf = xpad[:, T:]
    cb = c.reshape(B, T, LRU_HEADS, LRU_BLOCK)
    r = jax.nn.sigmoid(jnp.einsum('bthi,hij->bthj', cb, w_a).reshape(B, T, LRU_WIDTH) + b_a)
    i = jax.nn.sigmoid(jnp.einsum('bthi,hij->bthj', cb, w_x).reshape(B, T, LRU_WIDTH) + b_x)
    log_a = -LRU_C * r.astype(jnp.float32) * jax.nn.softplus(-lam.astype(jnp.float32))
    a = jnp.exp(log_a)
    b = jnp.sqrt(-jnp.expm1(2.0 * log_a)) * (i * c).astype(jnp.float32)

    def step(h, ab):
        a_t, b_t = ab
        h = a_t * h + b_t
        return h, h

    hT, hs = lax.scan(step, h0.astype(jnp.float32), (jnp.swapaxes(a, 0, 1), jnp.swapaxes(b, 0, 1)))
    return jnp.swapaxes(hs, 0, 1).astype(xl.dtype), new_buf, hT.astype(h0.dtype)

def hier_moe(x, w_rg, b_rg, w_re, b_re, wg, wu, wd):
    T = x.shape[0]
    lg = (x @ w_rg).astype(jnp.float32) + b_rg.astype(jnp.float32)
    pg = jax.nn.softmax(lg, axis=-1)
    g_idx = jnp.argmax(lg, axis=-1)
    pg_sel = jnp.take_along_axis(pg, g_idx[:, None], axis=1)[:, 0]
    le = ((x @ w_re).astype(jnp.float32) + b_re.astype(jnp.float32)).reshape(T, N_GROUPS, EXPERTS_PER_GROUP)
    le_sel = jnp.take_along_axis(le, g_idx[:, None, None], axis=1)[:, 0]
    pe = jax.nn.softmax(le_sel, axis=-1)
    top_v, top_i = lax.top_k(pe, TOP_K)
    top_v = top_v / jnp.sum(top_v, axis=-1, keepdims=True)
    w_e = jnp.sum(jax.nn.one_hot(top_i, EXPERTS_PER_GROUP, dtype=jnp.float32) * top_v[..., None], axis=1)
    comb = (jax.nn.one_hot(g_idx, N_GROUPS, dtype=jnp.float32)[:, :, None]
            * (pg_sel[:, None] * w_e)[:, None, :]).astype(x.dtype)
    y = jnp.zeros_like(x)
    for g in range(N_GROUPS):
        hg = jnp.einsum('td,edf->tef', x, wg[g])
        hu = jnp.einsum('td,edf->tef', x, wu[g])
        hh = jax.nn.silu(hg) * hu * comb[:, g, :, None]
        y = y + jnp.einsum('tef,efd->td', hh, wd[g])
    return y

def merge_and_ffn(x, attn, lru_h, yg, gn_attn, gn_lru, w_out, ln2_g, w_rg, b_rg, w_re, b_re, wg, wu, wd):
    lru_out = jax.nn.gelu(yg) * lru_h
    m = jnp.concatenate([rmsnorm(attn, gn_attn), rmsnorm(lru_out, gn_lru)], axis=-1)
    x = x + m @ w_out
    B, T, D = x.shape
    f = hier_moe(rmsnorm(x, ln2_g).reshape(B * T, D), w_rg, b_rg, w_re, b_re, wg, wu, wd)
    return x + f.reshape(B, T, D)

def setup_inputs(seed: int = 0) -> dict:
    key = jax.random.key(seed)
    ks = iter(jax.random.split(key, 32))
    f32 = jnp.float32
    nrm = lambda shape, s: jax.random.normal(next(ks), shape, f32) * s
    buf = min(WINDOW, PAST_LEN)
    a0 = jax.random.uniform(next(ks), (DEPTH, LRU_WIDTH), f32, 0.9, 0.999)
    return {
        "x_prompt": nrm((BATCH, SEQ, D_MODEL), 1.0),
        "x_sample": nrm((DEC_BATCH, DEC_SEQ, D_MODEL), 1.0),
        "cache_k_win": nrm((DEPTH, DEC_BATCH, buf, N_KV_HEADS, HEAD_DIM), 1.0),
        "cache_v_win": nrm((DEPTH, DEC_BATCH, buf, N_KV_HEADS, HEAD_DIM), 1.0),
        "state_conv": nrm((DEPTH, DEC_BATCH, CONV_WIDTH - 1, LRU_WIDTH), 1.0),
        "state_lru_h": nrm((DEPTH, DEC_BATCH, LRU_WIDTH), 0.5),
        "ln1_g": 1.0 + nrm((DEPTH, D_MODEL), 0.05),
        "w_in": nrm((DEPTH, D_MODEL, IN_WIDTH), D_MODEL ** -0.5),
        "w_conv": nrm((DEPTH, CONV_WIDTH, LRU_WIDTH), CONV_WIDTH ** -0.5),
        "b_conv": nrm((DEPTH, LRU_WIDTH), 0.01),
        "w_rg_a": nrm((DEPTH, LRU_HEADS, LRU_BLOCK, LRU_BLOCK), LRU_BLOCK ** -0.5),
        "b_rg_a": nrm((DEPTH, LRU_WIDTH), 0.01),
        "w_rg_x": nrm((DEPTH, LRU_HEADS, LRU_BLOCK, LRU_BLOCK), LRU_BLOCK ** -0.5),
        "b_rg_x": nrm((DEPTH, LRU_WIDTH), 0.01),
        "lru_lambda": jnp.log(a0) - jnp.log1p(-a0),
        "attn_sinks": nrm((DEPTH, N_HEADS), 0.5),
        "gn_attn": 1.0 + nrm((DEPTH, ATTN_WIDTH), 0.05),
        "gn_lru": 1.0 + nrm((DEPTH, LRU_WIDTH), 0.05),
        "w_out": nrm((DEPTH, ATTN_WIDTH + LRU_WIDTH, D_MODEL), (ATTN_WIDTH + LRU_WIDTH) ** -0.5),
        "ln2_g": 1.0 + nrm((DEPTH, D_MODEL), 0.05),
        "w_router_grp": nrm((DEPTH, D_MODEL, N_GROUPS), D_MODEL ** -0.5),
        "b_router_grp": nrm((DEPTH, N_GROUPS), 0.01),
        "w_router_exp": nrm((DEPTH, D_MODEL, N_GROUPS * EXPERTS_PER_GROUP), D_MODEL ** -0.5),
        "b_router_exp": nrm((DEPTH, N_GROUPS * EXPERTS_PER_GROUP), 0.01),
        "w_exp_gate": nrm((DEPTH, N_GROUPS, EXPERTS_PER_GROUP, D_MODEL, D_EXPERT), D_MODEL ** -0.5),
        "w_exp_up": nrm((DEPTH, N_GROUPS, EXPERTS_PER_GROUP, D_MODEL, D_EXPERT), D_MODEL ** -0.5),
        "w_exp_down": nrm((DEPTH, N_GROUPS, EXPERTS_PER_GROUP, D_EXPERT, D_MODEL), D_EXPERT ** -0.5),
        "final_g": 1.0 + nrm((D_MODEL,), 0.05),
    }

def reference(x_prompt, x_sample, cache_k_win, cache_v_win, state_conv, state_lru_h,
              ln1_g, w_in, w_conv, b_conv, w_rg_a, b_rg_a, w_rg_x, b_rg_x, lru_lambda,
              attn_sinks, gn_attn, gn_lru, w_out, ln2_g, w_router_grp, b_router_grp,
              w_router_exp, b_router_exp, w_exp_gate, w_exp_up, w_exp_down, final_g):
    hp, hs = x_prompt, x_sample
    B, T, _ = x_prompt.shape
    DB, Tq, _ = x_sample.shape
    p_k, p_v, p_c, p_h, s_k, s_v, s_c, s_h = [], [], [], [], [], [], [], []
    for l in range(DEPTH):
        lru_w = (w_conv[l], b_conv[l], w_rg_a[l], b_rg_a[l], w_rg_x[l], b_rg_x[l], lru_lambda[l])
        tail_w = (gn_attn[l], gn_lru[l], w_out[l], ln2_g[l], w_router_grp[l], b_router_grp[l],
                  w_router_exp[l], b_router_exp[l], w_exp_gate[l], w_exp_up[l], w_exp_down[l])
        q, k, v, xl, yg = in_proj(hp, ln1_g[l], w_in[l])
        pos = jnp.arange(T)
        attn, kw, vw = swa_prompt(rotary(q, pos), rotary(k, pos), v, attn_sinks[l])
        conv0 = jnp.zeros((B, CONV_WIDTH - 1, LRU_WIDTH), xl.dtype)
        h0 = jnp.zeros((B, LRU_WIDTH), xl.dtype)
        lru_h, cbuf, hT = rglru(xl, conv0, h0, *lru_w)
        hp = merge_and_ffn(hp, attn, lru_h, yg, *tail_w)
        p_k.append(kw); p_v.append(vw); p_c.append(cbuf); p_h.append(hT)
        q, k, v, xl, yg = in_proj(hs, ln1_g[l], w_in[l])
        pos = PAST_LEN + jnp.arange(Tq)
        attn, kw, vw = swa_sample(rotary(q, pos), rotary(k, pos), v, cache_k_win[l], cache_v_win[l], attn_sinks[l])
        lru_h, cbuf, hT = rglru(xl, state_conv[l], state_lru_h[l], *lru_w)
        hs = merge_and_ffn(hs, attn, lru_h, yg, *tail_w)
        s_k.append(kw); s_v.append(vw); s_c.append(cbuf); s_h.append(hT)
    y_prompt = rmsnorm(hp, final_g)
    y_sample = rmsnorm(hs, final_g)
    return (y_prompt, y_sample, jnp.stack(p_k), jnp.stack(p_v), jnp.stack(p_c), jnp.stack(p_h),
            jnp.stack(s_k), jnp.stack(s_v), jnp.stack(s_c), jnp.stack(s_h))


_drawn_inputs = setup_inputs


def setup_inputs(seed=0):
    import zlib

    import numpy as np

    out = dict(_drawn_inputs(seed))
    spreads = {}
    factors = {'b_rg_a': 25.094,
     'b_rg_x': 8.0,
     'attn_sinks': 8.0,
     'b_router_grp': 36.637,
     'b_router_exp': 4.492}
    for name, (base, spread) in spreads.items():
        noise = np.random.default_rng([zlib.crc32(name.encode()), seed]).standard_normal(out[name].shape)
        drawn = base * np.exp(spread * noise) if base else spread * noise
        out[name] = __import__('jax').numpy.asarray(drawn.astype(out[name].dtype))
    for name, factor in factors.items():
        out[name] = (out[name] * factor).astype(out[name].dtype)
    return out
```

```python
from contextlib import ExitStack

import numpy as np

import concourse.bass as bass
from concourse import mybir

F32 = mybir.dt.float32
BF16 = mybir.dt.bfloat16
I32 = mybir.dt.int32
U32 = mybir.dt.uint32
ALU = mybir.AluOpType
ACT = mybir.ActivationFunctionType
AX_X = mybir.AxisListType.X
ds = bass.ds

P = 128
D_MODEL = 1024
KD = D_MODEL // P
SEQ = 1024
NDEC = 8
TOKENS = SEQ + NDEC
NPT = SEQ // P
NT = NPT + 1
HEAD_DIM = 64
N_HEADS = 8
N_KV = 2
WINDOW = 128
ATTN = N_HEADS * HEAD_DIM
KV = N_KV * HEAD_DIM
QKV = ATTN + 2 * KV
LRU = D_MODEL - ATTN
NFT = LRU // P
CONV = 4
CHUNK = TOKENS // 3
PAST_LEN = 2048
N_GROUPS = 4
N_PER_GROUP = 8
NE = N_GROUPS * N_PER_GROUP
NR = N_GROUPS + NE
D_EXPERT = D_MODEL // 4
KF = D_EXPERT // P
TOPK = 2
CAP = P
MAXC = -(-TOKENS // CAP)
MAXV = TOPK * TOKENS // CAP
EPS = 1e-6
MASKED = -1e30
NOROW = 1 << 20
GELU_C = 0.7978845608028654
GELU_A = 0.044715

C_W, C_B, C_BA, C_BX, C_LAM, C_GN, C_ST, C_H0 = 0, 4, 5, 6, 7, 8, 9, 33
C_N = 41
O_XS, O_HS, O_XL, O_HL, O_N = 0, 8, 16, 19, 20
K_ID, K_UP, K_MASK, K_CS, K_THR, K_IE, K_IV, K_VALID = 0, 128, 256, 1280, 1856, 1864, 1896, 1912
K_N = 1912 + NT


class Count:

    def __init__(self):
        self.base, self.n = 0, 0

    def up(self):
        self.n += 1
        return 1

    def now(self):
        return self.base + self.n

    def at(self, base):
        self.base, self.n = base, 0


def build(nc, a):
    xtab = nc.dram_tensor("xtab", (NT * P, D_MODEL), F32).ap()
    ypair = nc.dram_tensor("ypair", (TOPK * TOKENS, D_MODEL), F32).ap()
    rowlist = nc.dram_tensor("rowlist", (CAP * NE * MAXC, 2), I32).ap()
    vnew = nc.dram_tensor("vnew", (NDEC, KV), F32).ap()

    with ExitStack() as ctx:
        def sb(name, shape, dt=F32):
            return ctx.enter_context(nc.sbuf_tensor(name, shape, dt))

        def sem(name):
            return ctx.enter_context(nc.semaphore(name))

        class Region:

            def __init__(self, name, words):
                self.t, self.words, self.at = sb(name, [P, words]), words, 0

            def cut(self, *shape):
                n = int(np.prod(shape))
                v = self.t[:, self.at:self.at + n]
                self.at += n
                assert self.at <= self.words, (self.at, self.words)
                if len(shape) == 2:
                    v = v.rearrange("p (a b) -> p a b", a=shape[0])
                if len(shape) == 3:
                    v = v.rearrange("p (a b c) -> p a b c", a=shape[0], b=shape[1])
                return v

            def phase(self, at=0):
                self.at = at

        PS = ctx.enter_context(nc.psum_tensor("PS", [P, 8, 512], F32))

        cst = sb("cst", [P, K_N])
        ones = sb("ones", [P, P])
        mhalf = sb("mhalf", [P, 1])
        g1 = sb("g1", [P, KD])
        gna = sb("gna", [P, NFT])
        sinkb = sb("sinkb", [P, N_HEADS])
        sinkc = sb("sinkc", [N_HEADS, 1])
        chp = sb("chp", [P, NFT, C_N])
        drv = sb("drv", [P, NFT, 3])
        wr = sb("wr", [P, KD, NR])
        brb = sb("brb", [P, NR])
        payload = sb("payload", [P, NT, 4], I32)
        stat = sb("stat", [P, 12, NT])
        ssx, varx, rsx, ssa, ssl, val, ral, ss2, var2, rs2 = (stat[:, i, :] for i in range(10))
        ss3, rs3 = stat[:, 10, :], stat[:, 11, :]
        val2 = sb("val2", [P, 2, NT])
        comb = sb("comb", [P, NT, 2])
        xin = sb("xin", [P, 2, D_MODEL])
        rot = sb("rot", [P, 2, ATTN + KV])
        smo = sb("smo", [P, NFT, O_N])
        ident = cst[:, K_ID:K_ID + P]
        upper = cst[:, K_UP:K_UP + P]

        RA = Region("RA", KD * NT * P)
        xT_all = RA.cut(KD, NT * P)
        RA.phase()
        x2_all = RA.cut(NT, D_MODEL)

        RB = Region("RB", KD * NT * P)
        mT_all = RB.cut(KD, NT * P)
        RB.phase(NFT * NT * P)
        PT = RB.cut(4, 512)
        t1 = RB.cut(ATTN + KV)
        t2 = RB.cut(ATTN + KV)

        WXP = KD * D_EXPERT * 2 + KF * D_MODEL
        RC = Region("RC", KD * D_MODEL)
        wqkv = RC.cut(KD, QKV)
        wxy1 = RC.cut(KD, 2 * P)
        RC.phase()
        wout = RC.cut(KD, D_MODEL)
        RC.phase()
        wexp1 = RC.cut(WXP)

        RE = Region("RE", 9900)
        wxy0 = RE.cut(KD, 2 * P)
        wgate = RE.cut(2, 2 * P)
        v_all = RE.cut(NT + 1, KV)
        kT_all = RE.cut((NT + 1) * P)
        rbc = RE.cut(NT * P)
        kTs = RE.cut(NDEC, P)
        Vs = RE.cut(NDEC, P)
        Qs = RE.cut(NDEC, N_HEADS)
        cp = RE.cut(C_N)
        dv = RE.cut(3)
        RE.phase()
        wexp0 = RE.cut(WXP)
        wxy = [wxy0, wxy1]
        wexp = [wexp0, wexp1]

        RD = Region("RD", 9240)
        E = RD.cut(4, 512)
        qz = RD.cut(2, N_HEADS, P)
        xs = RD.cut(2, KD, P)
        u_sb = RD.cut(ATTN + KV)
        at_st = RD.cut(ATTN)
        rs = RD.cut(N_HEADS)
        mx = RD.cut(N_HEADS)
        nm = RD.cut(N_HEADS)
        dsink = RD.cut(N_HEADS)
        es = RD.cut(N_HEADS)
        den = RD.cut(N_HEADS)
        rinv = RD.cut(N_HEADS)
        RD.phase()
        xlb = RD.cut(CONV - 1 + TOKENS)
        cT = RD.cut(TOKENS)
        yb = RD.cut(TOKENS)
        inn = RD.cut(TOKENS)
        trs = xlb[:, CONV - 1:]
        tib = RD.cut(TOKENS)
        wv = RD.cut(TOKENS)
        sqh = RD.cut(TOKENS)
        sqacc = RD.cut(TOKENS)
        sqb = inn
        sm8 = RD.cut(4, 8)
        sa_mx = RD.cut(8)
        sa_es = RD.cut(8)
        sa_sum = RD.cut(8)
        RD.phase()
        saS = RD.cut(NDEC * P)
        saP = RD.cut(NDEC * N_HEADS)
        saT = RD.cut(NFT, NDEC)
        RD.phase()
        xn = RD.cut(2, D_MODEL)
        xT2 = RD.cut(KD, P)
        mTs = RD.cut(2, KD, P)
        g2b = RD.cut(D_MODEL)
        x2t = RD.cut(512)
        lg = RD.cut(8)
        le = RD.cut(NE)
        top = RD.cut(8)
        eg = RD.cut(4)
        ohg = RD.cut(4)
        lem = RD.cut(N_PER_GROUP, N_GROUPS)
        les = RD.cut(8)
        toe = RD.cut(8)
        sc = RD.cut(16)
        oh = RD.cut(2, NE)
        cnt = RD.cut(NE)
        M = RD.cut(NE)
        rk = RD.cut(NE)
        thrq = RD.cut(2, 8)
        rr = RD.cut(4, 2)
        jnk32 = RD.cut(2, NE)
        bigc = RD.cut(NE, 8)
        xe = RD.cut(NE)
        incl = RD.cut(NE)
        lev = RD.cut(MAXV, NE)
        lex = RD.cut(MAXV, NE)
        ev = RD.cut(2, MAXV)
        RD.phase()
        xg = RD.cut(2, D_MODEL)
        xgT = RD.cut(2, KD, P)
        hh = RD.cut(2, D_EXPERT)
        hT = RD.cut(2, KF, P)
        yo = RD.cut(2, D_MODEL)
        RD.phase()
        yp = RD.cut(2, TOPK * D_MODEL)
        ob = RD.cut(2, D_MODEL)
        gfb = RD.cut(D_MODEL)
        junk = sb("junk", [P, D_MODEL], BF16)
        idxg = sb("idxg", [P, 8], U32)
        idxp = sb("idxp", [P, 8], U32)
        idxs = sb("idxs", [P, 2, 2], U32)
        pays = sb("pays", [P, 2, 4], I32)
        lists = sb("lists", [P, NE * MAXC, 2], I32)
        pidg = sb("pidg", [P, 2, 1], I32)
        pids = sb("pids", [P, 2, 1], I32)
        vtab = sb("vtab", [1, 2 * MAXV + 2], I32)

        cst_in = sem("cst_in")
        par_in = sem("par_in")
        wqkv_in = sem("wqkv_in")
        mem0 = sem("mem0")
        x_sq = sem("x_sq")
        x_var = sem("x_var")
        x_rstd = sem("x_rstd")
        xT_ps = sem("xT_ps")
        xs_ok = sem("xs_ok")
        xTall_ok = sem("xTall_ok")
        s_ps = sem("s_ps")
        nmax_ok = sem("nmax_ok")
        exp_ok = sem("exp_ok")
        es_ok = sem("es_ok")
        qkv_ps = sem("qkv_ps")
        u_ok = sem("u_ok")
        v_ok = sem("v_ok")
        pt_ps = sem("pt_ps")
        pta_ok = sem("pta_ok")
        ptd_ok = sem("ptd_ok")
        o_ps = sem("o_ps")
        rot_ok = sem("rot_ok")
        qkT_ps = sem("qkT_ps")
        qz_ok = sem("qz_ok")
        kT_ok = sem("kT_ok")
        attn_ok = sem("attn_ok")
        aT_ps = sem("aT_ps")
        aT_ok = sem("aT_ok")
        ssa_ok = sem("ssa_ok")
        drv_ok = sem("drv_ok")
        expl_ok = sem("expl_ok")
        diag_ok = sem("diag_ok")
        rbc_ps = sem("rbc_ps")
        rbc_ok = sem("rbc_ok")
        xl_ps = sem("xl_ps")
        yg_ps = sem("yg_ps")
        gt_ps = sem("gt_ps")
        xl_ok = sem("xl_ok")
        conv_ok = sem("conv_ok")
        y_ok = sem("y_ok")
        gate_ok = sem("gate_ok")
        s_ok = sem("s_ok")
        y2_ok = sem("y2_ok")
        inn_ok = sem("inn_ok")
        th_ok = sem("th_ok")
        sqrt_ok = sem("sqrt_ok")
        lru_ok = sem("lru_ok")
        sqb_ok = sem("sqb_ok")
        sqacc_ok = sem("sqacc_ok")
        cp_ok = sem("cp_ok")
        pre_in = sem("pre_in")
        vnew_out = sem("vnew_out")
        vnew_in = sem("vnew_in")
        sa_q = sem("sa_q")
        sa_s = sem("sa_s")
        sa_e = sem("sa_e")
        sa_sx = sem("sa_sx")
        sa_n = sem("sa_n")
        sa_pt = sem("sa_pt")
        sa_pte = sem("sa_pte")
        sa_pv = sem("sa_pv")
        sa_m = sem("sa_m")
        sa_sq = sem("sa_sq")
        ss_ps = sem("ss_ps")
        ssl_ok = sem("ssl_ok")
        varal_ok = sem("varal_ok")
        ral_ok = sem("ral_ok")
        smo_out = sem("smo_out")
        kwin_out = sem("kwin_out")
        vwin_out = sem("vwin_out")
        kv_dec = sem("kv_dec")
        wout_in = sem("wout_in")
        op_ps = sem("op_ps")
        x2_ok = sem("x2_ok")
        ss2_ok = sem("ss2_ok")
        var2_ok = sem("var2_ok")
        rs2_ok = sem("rs2_ok")
        xn_ok = sem("xn_ok")
        xT2_ps = sem("xT2_ps")
        xT2a_ok = sem("xT2a_ok")
        xT2d_ok = sem("xT2d_ok")
        r_ps = sem("r_ps")
        lgx_ok = sem("lgx_ok")
        ege_ok = sem("ege_ok")
        top_ok = sem("top_ok")
        eexp_ok = sem("eexp_ok")
        M_ok = sem("M_ok")
        rk_ps = sem("rk_ps")
        idx_ok = sem("idx_ok")
        pay_ok = sem("pay_ok")
        lists_init = sem("lists_init")
        lists_in = sem("lists_in")
        mts_ok = sem("mts_ok")
        cnt_ok = sem("cnt_ok")
        vtab_ok = sem("vtab_ok")
        passed = sem("passed")
        xgT_ps = sem("xgT_ps")
        xga_ok = sem("xga_ok")
        xgd_ok = sem("xgd_ok")
        gu_ps = sem("gu_ps")
        th2_ok = sem("th2_ok")
        h_ok = sem("h_ok")
        hT_ps = sem("hT_ps")
        hTa_ok = sem("hTa_ok")
        y_ps = sem("y_ps")
        yoa_ok = sem("yoa_ok")
        yod_ok = sem("yod_ok")
        pidg_ok = sem("pidg_ok")
        pids_ok = sem("pids_ok")
        x3_ok = sem("x3_ok")
        ss3_ok = sem("ss3_ok")
        var3_ok = sem("var3_ok")
        rs3_ok = sem("rs3_ok")
        ob_ok = sem("ob_ok")
        gm0 = sem("gm0")
        dve_done = sem("dve_done")
        pool_done = sem("pool_done")
        g_free = sem("g_free")
        x3a = sem("x3a")
        gf_in = sem("gf_in")
        x_in = [sem("x_in0"), sem("x_in1")]
        x_in2 = [sem("x_in2_0"), sem("x_in2_1")]
        wxy_in = [sem("wxy_in0"), sem("wxy_in1")]
        xt_out = [sem("xt_out0"), sem("xt_out1")]
        scat = [sem("scat0"), sem("scat1")]
        wexp_in = [sem("wexp_in0"), sem("wexp_in1")]
        xg_in = [sem("xg_in0"), sem("xg_in1")]
        yo_out = [sem("yo_out0"), sem("yo_out1")]
        yp_in = [sem("yp_in0"), sem("yp_in1")]
        o_out = [sem("o_out0"), sem("o_out1")]

        block = ctx.enter_context(nc.Block())

        def alone(eng):
            eng.sem_inc(passed, 1)

        @block.sync
        def _(sp):
            def load_x(t, p, rows, sems):
                sp.dma_start(xin[0:rows, p, :], a["x"][ds(t * P, rows), :]).then_inc(sems[p], 16)

            sp.dma_start(cst[:, :], a["cst"]).then_inc(cst_in, 16)
            load_x(0, 0, P, x_in)
            for dst, name in ((g1[:, :], "g1"), (gna[:, :], "gna"), (sinkc[:, :], "sinkc"), (chp[:, :, :], "chp"),
                              (wr[:, :, :], "wr"), (payload[:, :, :], "payload"), (kTs, "kTs"), (Vs, "Vs")):
                sp.dma_start(dst, a[name]).then_inc(par_in, 16)
            sp.dma_start(sinkb[:, :], a["sinks"].partition_broadcast(P)).then_inc(par_in, 16)
            sp.dma_start(brb[:, :], a["b_router"].partition_broadcast(P)).then_inc(par_in, 16)
            sp.dma_start(wqkv, a["wqkv"]).then_inc(wqkv_in, 16)
            load_x(1, 1, P, x_in)
            sp.dma_start(a["s_k"][:, 0:WINDOW - 1, :], a["cache_k"][:, 1:WINDOW, :]).then_inc(kv_dec, 16)
            sp.dma_start(a["s_v"][:, 0:WINDOW - 1, :], a["cache_v"][:, 1:WINDOW, :]).then_inc(kv_dec, 16)
            sp.dma_start(a["s_c"], a["conv_old"][:, 1:CONV - 1, :]).then_inc(kv_dec, 16)

            def reload_x(t, p, rows):
                sp.wait_ge(xT_ps, 2 * t - 2)
                alone(sp)
                sp.wait_ge(x_sq, t - 1)
                load_x(t, p, rows, x_in)

            with sp.Fori(0, 3) as j:
                reload_x(2 * j + 2, 0, P)
                reload_x(2 * j + 3, 1, P)
            reload_x(8, 0, NDEC)

            def load_wxy(f, p):
                sp.dma_start(wxy[p], a["wxy"][f]).then_inc(wxy_in[p], 16)
                sp.dma_start(wgate[:, p, :], a["wgate"][f]).then_inc(wxy_in[p], 16)
            for f in range(2):
                load_wxy(f, f)
            sp.wait_ge(rot_ok, NT)
            sp.wait_ge(v_ok, NT)
            sp.dma_start(a["p_k"], rot[:, 1, ATTN:]).then_inc(kwin_out, 16)
            sp.dma_start(a["p_v"], v_all[:, NPT, :]).then_inc(kwin_out, 16)
            sp.dma_start(a["s_k"][:, WINDOW - 1, :], rot[0:NDEC, 0, ATTN:]).then_inc(kwin_out, 16)
            sp.dma_start(a["s_v"][:, WINDOW - 1, :], v_all[0:NDEC, NT, :]).then_inc(kwin_out, 16)
            sp.dma_start(vnew, v_all[0:NDEC, NT, :]).then_inc(vnew_out, 16)
            sp.wait_ge(vnew_out, 16)
            sp.wait_ge(par_in, 16 * 10)
            sp.dma_start(Vs[0:1, :, :], vnew.rearrange("(o b) d -> o b d", o=1)).then_inc(vnew_in, 16)
            for p in range(2):
                sp.wait_ge(yg_ps, 3 * (p + 1))
                sp.wait_ge(gt_ps, 6 * (p + 1))
                if p == 0:
                    sp.wait_ge(wxy_in[0], 32)
                load_wxy(2 + p, p)
            sp.wait_ge(yg_ps, 12)
            sp.wait_ge(qkv_ps, NT)
            sp.dma_start(wout, a["wout"]).then_inc(wout_in, 16)
            sp.wait_ge(lru_ok, NFT + 1)
            sp.dma_start(a["rec"], smo[:, :, :]).then_inc(smo_out, 16)
            sp.wait_ge(aT_ps, NPT + 1)
            sp.wait_ge(ss_ps, 1)
            sp.dma_start(g2b, a["g2"].partition_broadcast(P)).then_inc(pre_in, 16)
            sp.wait_ge(sa_pv, NDEC)
            sp.wait_ge(vnew_out, 16)
            sp.wait_ge(kwin_out, 64)
            sp.dma_start(wexp[0], a["wexp"][0]).then_inc(wexp_in[0], 16)

            load_x(0, 0, P, x_in2)
            load_x(1, 1, P, x_in2)

            def step3(t, p, rows):
                sp.wait_ge(xn_ok, t + 1)
                sp.dma_start(xtab[ds(t * P, P), :], xn[:, p, :]).then_inc(xt_out[p], 16)
                if rows:
                    sp.wait_ge(x2_ok, 2 * t + 2)
                    load_x(t + 2, p, rows, x_in2)

            with sp.Fori(0, 3) as j:
                step3(2 * j, 0, P)
                step3(2 * j + 1, 1, P)
            step3(6, 0, NDEC)
            step3(7, 1, 0)
            step3(8, 0, 0)

            sp.wait_ge(op_ps, 2 * NT)
            sp.dma_start(wexp[1], a["wexp"][1]).then_inc(wexp_in[1], 16)
            with sp.Fori(0, NE // 2 - 1) as j:
                for p in range(2):
                    sp.wait_ge(y_ps, 2 * (2 * j + p + 1))
                    sp.dma_start(wexp[p], a["wexp"][ds(2 * j + p + 2, 1)].rearrange("o p n -> (o p) n"))\
                      .then_inc(wexp_in[p], 16)
            sp.wait_ge(vtab_ok, 1)
            nv = sp.value_load(vtab[0:1, 2 * MAXV:2 * MAXV + 1], min_val=0, max_val=MAXV)
            with sp.If(nv > 0):
                with sp.Fori(0, nv) as v:
                    e = sp.value_load(vtab[0:1, ds(v, 1)], min_val=0, max_val=NE - 1)
                    sp.wait_ge(y_ps, 2 * v + 2 * NE)
                    sp.dma_start(wexp[0], a["wexp"][ds(e, 1)].rearrange("o p n -> (o p) n")).then_inc(wexp_in[0], 16)
                sp.wait_ge(vtab_ok, 1)
            sp.wait_ge(g_free, 1)

            def load_y(t, p, rows):
                sp.dma_start(yp[0:rows, p, :], ypair[ds(2 * t * P, 2 * rows), :].rearrange("(q two) d -> q (two d)", two=2))\
                  .then_inc(yp_in[p], 16)
            sp.dma_start(gfb, a["gf"].partition_broadcast(P)).then_inc(gf_in, 16)
            load_y(0, 0, P)
            load_y(1, 1, P)

            def store_y(t, p, rows):
                sp.wait_ge(ob_ok, t + 1)
                sp.dma_start(a["y"][ds(t * P, rows), :], ob[0:rows, p, :]).then_inc(o_out[p], 16)

            def step5(t, p, rows):
                sp.wait_ge(x3_ok, t + 1)
                load_y(t + 2, p, rows)
                store_y(t, p, P)
            with sp.Fori(0, 3) as j:
                step5(2 * j, 0, P)
                step5(2 * j + 1, 1, P)
            step5(6, 0, NDEC)
            store_y(7, 1, P)
            store_y(8, 0, NDEC)
            sp.wait_ge(o_out[0], 16 * 5)
            sp.wait_ge(o_out[1], 16 * 4)
            sp.wait_ge(kwin_out, 64)
            sp.wait_ge(kv_dec, 48)
            sp.wait_ge(smo_out, 16)
            sp.wait_ge(vnew_in, 16)

        @block.gpsimd
        def _(pool):
            for first_pass in (xTall_ok,):
                pool.sem_inc(first_pass, 1)
            pool.memset(mhalf[:, :], -0.5).then_inc(mem0, 1)
            pool.memset(ones[:, :], 1.0).then_inc(mem0, 1)
            pool.memset(stat[:, :, :], 1.0).then_inc(mem0, 1)

            pool.memset(qz, 0.0).then_inc(mem0, 1)
            pool.memset(kT_all[:, 0:P], 0.0).then_inc(mem0, 1)
            pool.memset(v_all[:, 0, :], 0.0).then_inc(mem0, 1)
            pool.memset(mT_all[:, 0:NFT, SEQ:], 0.0).then_inc(mem0, 1)
            pool.memset(lists[:, :, :], NOROW).then_inc(gm0, 1)
            pool.wait_ge(gm0, 1)
            pool.dma_start(rowlist.rearrange("(p n) c -> p n c", p=CAP), lists[:, :, :]).then_inc(lists_init, 16)

            def root(out, var, signal):
                nc.gpsimd.tensor_tensor(out, var, mhalf[:, 0:1], ALU.pow).then_inc(signal, 1)

            pool.wait_ge(mem0, 7)
            def tile1(t, p):
                pool.wait_ge(xs_ok, 2 * t + 2)
                nc.gpsimd.tensor_copy(xT_all[:, :, ds(t * P, P)], xs[:, p]).then_inc(xTall_ok, 1)
                pool.wait_ge(x_var, t + 1)
                root(rsx[:, ds(t, 1)], varx[:, ds(t, 1)], x_rstd)
            tile1(0, 0)
            with pool.Fori(0, 4) as j:
                tile1(2 * j + 1, 1)
                tile1(2 * j + 2, 0)

            pool.wait_ge(aT_ps, NPT + 1)
            pool.wait_ge(qkT_ps, 2 * NT)
            pool.wait_ge(attn_ok, NPT)
            pool.wait_ge(ssa_ok, NPT + 1)
            pool.wait_ge(rbc_ps, 1)
            pool.memset(sqacc, 0.0).then_inc(pool_done, 1)
            with pool.Fori(0, NFT) as f:
                pool.wait_ge(y2_ok, f + 1)
                alone(pool)
                nc.gpsimd.tensor_scalar(inn, inn, GELU_A, 1.0, ALU.mult, ALU.add).then_inc(pool_done, 1)
                pool.wait_ge(pool_done, 2 * f + 2)
                nc.gpsimd.tensor_tensor(inn, inn, yb, ALU.mult).then_inc(inn_ok, 1)
                pool.wait_ge(sqb_ok, f + 2)
                nc.gpsimd.tensor_tensor(sqacc, sqacc, sqb, ALU.add).then_inc(pool_done, 1)
                pool.wait_ge(pool_done, 2 * f + 3)
            pool.memset(junk[:, 0:2], 0.0).then_inc(sqacc_ok, 1)

            pool.wait_ge(varal_ok, 1)
            nc.gpsimd.tensor_tensor(ral, val, mhalf[:, 0:1].to_broadcast([P, NT]), ALU.pow).then_inc(ral_ok, 1)
            nc.gpsimd.tensor_tensor(val2[:, 1, :], val2[:, 0, :], mhalf[:, 0:1].to_broadcast([P, NT]), ALU.pow)\
              .then_inc(ral_ok, 1)

            def stage(t, p):
                if not isinstance(t, int) or t >= 2:
                    pool.wait_ge(op_ps, 2 * t - 2)
                nc.gpsimd.tensor_copy(mTs[:, p], mT_all[:, :, ds(t * P, P)]).then_inc(mts_ok, 1)

            def root2(t):
                pool.wait_ge(var2_ok, t + 1)
                root(rs2[:, ds(t, 1)], var2[:, ds(t, 1)], rs2_ok)

            def scatter(t, p, rows):
                pool.wait_ge(idx_ok, t + 1)
                nc.gpsimd.tensor_copy(pays[:, p, :], payload[:, ds(t, 1), :].rearrange("q o c -> q (o c)"))\
                  .then_inc(pay_ok, 1)
                pool.wait_ge(pay_ok, t + 1)
                alone(pool)
                for k in range(TOPK):
                    pool.indirect_dma_start(rowlist, bass.IndirectOffsetOnAxis(idxs[0:rows, p, k:k + 1], 0),
                                            pays[0:rows, p, 2 * k:2 * k + 2], None).then_inc(scat[p], 16)

            def scatter_done(p, rounds):
                pool.wait_ge(scat[p], 32 * rounds)

            pool.wait_ge(ss_ps, 1)
            pool.wait_ge(lru_ok, NFT + 1)
            pool.wait_ge(sa_m, 2)
            pool.wait_ge(lists_init, 16)
            stage(0, 0)
            stage(1, 1)
            root2(0)
            with pool.Fori(0, 3) as j:
                stage(2 * j + 2, 0)
                root2(2 * j + 1)
                scatter(2 * j, 0, P)
                scatter_done(0, j + 1)
                stage(2 * j + 3, 1)
                root2(2 * j + 2)
                scatter(2 * j + 1, 1, P)
                scatter_done(1, j + 1)
            stage(8, 0)
            root2(7)
            scatter(6, 0, P)
            scatter_done(0, 4)
            root2(8)
            scatter(7, 1, P)
            scatter_done(1, 4)
            scatter(8, 0, NDEC)
            scatter_done(0, 5)
            pool.dma_start(lists[:, :, :], rowlist.rearrange("(p n) c -> p n c", p=CAP)).then_inc(lists_in, 16)
            for p in range(2):
                pool.wait_ge(xt_out[p], 16 * (5 - p))
            pool.wait_ge(idx_ok, NT)
            pool.wait_ge(cnt_ok, 1)
            pool.memset(xg, 0.0).then_inc(gm0, 1)
            pool.wait_ge(gm0, 2)
            pool.wait_ge(lists_in, 16)

            def gather(n, col, p):
                if not (isinstance(n, int) and n < 2):
                    pool.wait_ge(xgT_ps, 2 * n - 2)
                nc.gpsimd.tensor_copy(pidg[:, p, :], lists[:, ds(col, 1), 0]).then_inc(pidg_ok, 1)
                pool.wait_ge(pidg_ok, n + 1)
                alone(pool)
                pool.indirect_dma_start(xg[:, p, :], None, xtab,
                                        bass.IndirectOffsetOnAxis(pidg[:, p, :].bitcast(U32), 0),
                                        bounds_check=TOKENS - 1, oob_is_err=False).then_inc(xg_in[p], 16)

            def spread(n, col, p, rounds):
                if not (isinstance(rounds, int) and rounds == 0):
                    pool.wait_ge(yo_out[p], 16 * rounds)
                nc.gpsimd.tensor_copy(pids[:, p, :], lists[:, ds(col, 1), 1]).then_inc(pids_ok, 1)
                pool.wait_ge(pids_ok, n + 1)
                pool.wait_ge(yoa_ok, n + 1)
                pool.wait_ge(yod_ok, n + 1)
                alone(pool)
                pool.indirect_dma_start(ypair, bass.IndirectOffsetOnAxis(pids[:, p, :].bitcast(U32), 0),
                                        yo[:, p, :], None,
                                        bounds_check=TOPK * TOKENS - 1, oob_is_err=False).then_inc(yo_out[p], 16)

            gather(0, 0, 0)
            gather(1, MAXC, 1)
            def pair(j):
                for p in range(2):
                    gather(2 * j + p + 2, (2 * j + p + 2) * MAXC, p)
                    spread(2 * j + p, (2 * j + p) * MAXC, p, j)
            pair(0)
            with pool.Fori(1, NE // 2 - 1) as j:
                pair(j)
            for p in range(2):
                spread(NE - 2 + p, (NE - 2 + p) * MAXC, p, NE // 2 - 1)
            for p in range(2):
                pool.wait_ge(yo_out[p], 16 * (NE // 2))
            pool.wait_ge(vtab_ok, 1)
            nv = pool.value_load(vtab[0:1, 2 * MAXV:2 * MAXV + 1], min_val=0, max_val=MAXV)
            with pool.If(nv > 0):
                with pool.Fori(0, nv) as v:
                    col = pool.value_load(vtab[0:1, ds(v + MAXV, 1)], min_val=0, max_val=NE * MAXC - 1)
                    pool.wait_ge(xgT_ps, 2 * v + 2 * NE)
                    gather(v + NE, col, 0)
                    spread(v + NE, col, 0, v + NE // 2)
                    pool.wait_ge(yo_out[0], 16 * v + 16 * (NE // 2 + 1))
                pool.wait_ge(vtab_ok, 1)
            pool.memset(junk[:, 0:2], 0.0).then_inc(g_free, 1)
            with pool.Fori(0, NT) as t:
                pool.wait_ge(var3_ok, t + 1)
                root(rs3[:, ds(t, 1)], ss3[:, ds(t, 1)], rs3_ok)

        @block.scalar
        def _(act):
            A = nc.scalar.activation
            for first_pass in (ssa_ok, aT_ok, gate_ok, s_ok, sqb_ok, ss2_ok, ss3_ok):
                act.sem_inc(first_pass, 1)

            act.wait_ge(expl_ok, 1)
            A(drv[:, :, 0], drv[:, :, 0], ACT.Exp, scale=-1.0).then_inc(drv_ok, 1)

            def step1(t, p, rounds, att):
                b = t - 1
                if att:
                    act.wait_ge(xTall_ok, t)
                for k in range(KD):
                    if k % 4 == 0:
                        act.wait_ge(xT_ps, 2 * t + 1 + k // 4)
                    o = A(xs[:, p, k, :], PS[:, 2 + k // 4, (k % 4) * P:(k % 4 + 1) * P], ACT.Copy, scale=g1[:, k:k + 1])
                    if k % 4 == 3:
                        o.then_inc(xs_ok, 1)
                act.wait_ge(x_in[p], 16 * rounds)
                if att:
                    act.wait_ge(x_sq, t)
                    act.wait_ge(ssa_ok, b + 1)
                A(junk[:, :], xin[:, p, :], ACT.Square, accum_out=ssx[:, ds(t, 1)]).then_inc(x_sq, 1)
                if att:
                    act.wait_ge(nmax_ok, b + 1)
                    for h in range(N_HEADS):
                        e = E[:, h // 2, (h % 2) * 256:(h % 2 + 1) * 256]
                        A(e, e, ACT.Exp, bias=nm[:, h:h + 1], accum_out=rs[:, h:h + 1]).then_inc(exp_ok, 1)
                    A(es, dsink, ACT.Exp).then_inc(es_ok, 1)
                    act.wait_ge(pt_ps, 4 * b + 2)
                    A(PT[:, 0, :], PS[:, 0, :], ACT.Copy).then_inc(pta_ok, 1)
                act.wait_ge(qkv_ps, t + 1)
                act.wait_ge(x_rstd, t + 1)
                if att:
                    act.wait_ge(rot_ok, t)
                A(u_sb[:, 0:ATTN], PS[:, 4, :], ACT.Copy, scale=rsx[:, ds(t, 1)])
                A(u_sb[:, ATTN:], PS[:, 5, 0:KV], ACT.Copy, scale=rsx[:, ds(t, 1)]).then_inc(u_ok, 1)
                A(v_all[:, ds(t + 1, 1), :], PS[:, 5, KV:2 * KV].rearrange("q (o c) -> q o c", o=1), ACT.Copy,
                  scale=rsx[:, ds(t, 1)]).then_inc(v_ok, 1)
                if att:
                    act.wait_ge(pt_ps, 4 * b + 4)
                    A(PT[:, 2, :], PS[:, 2, :], ACT.Copy).then_inc(pta_ok, 1)
                act.wait_ge(qkT_ps, 2 * t + 1)
                for lo in range(2):
                    half = slice(64 * lo, 64 * lo + 64)
                    o = A(qz[half, p, lo::2, :], PS[half, 7, :].rearrange("q (h c) -> q h c", h=4), ACT.Copy)
                o.then_inc(qz_ok, 1)
                if att:
                    act.wait_ge(attn_ok, b + 1)
                    act.wait_ge(x_sq, t + 1)
                    A(junk[:, 0:ATTN], at_st, ACT.Square, accum_out=ssa[:, ds(b, 1)]).then_inc(ssa_ok, 1)
                    act.wait_ge(aT_ps, b + 2)
                    for k in range(NFT):
                        o = A(mT_all[:, k, ds(b * P, P)], PS[:, 6, k * P:(k + 1) * P], ACT.Copy, scale=gna[:, k:k + 1])
                    o.then_inc(aT_ok, 1)

            act.wait_ge(par_in, 16 * 10)
            act.wait_ge(mem0, 7)
            step1(0, 0, 1, False)
            with act.Fori(0, 4) as j:
                step1(2 * j + 1, 1, j + 1, True)
                step1(2 * j + 2, 0, j + 2, True)

            act.wait_ge(rbc_ok, 1)
            with act.Fori(0, NFT) as f:
                for c in range(3):
                    cols = slice(c * CHUNK, (c + 1) * CHUNK)
                    act.wait_ge(gt_ps, 6 * f + 2 * c + 1)
                    if c == 0:
                        act.wait_ge(cp_ok, f + 1)
                    A(trs[:, cols], PS[:, 6, 0:CHUNK], ACT.Tanh, bias=dv[:, 0:1], scale=0.5).then_inc(gate_ok, 1)
                    act.wait_ge(gt_ps, 6 * f + 2 * c + 2)
                    A(tib[:, cols], PS[:, 7, 0:CHUNK], ACT.Tanh, bias=dv[:, 1:2], scale=0.5).then_inc(gate_ok, 1)
                act.wait_ge(gate_ok, 6 * f + 6 + 1)
                A(trs, trs, ACT.Tanh, bias=dv[:, 2:3], scale=dv[:, 2:3]).then_inc(s_ok, 1)
                act.wait_ge(y_ok, 3 * f + 4)
                act.wait_ge(pool_done, 2 * f + 1)
                A(inn, yb, ACT.Square).then_inc(y2_ok, 1)
                act.wait_ge(inn_ok, f + 1)
                A(inn, inn, ACT.Tanh, scale=GELU_C).then_inc(th_ok, 1)
                act.wait_ge(s_ok, f + 2)
                A(sqh, trs, ACT.Sqrt).then_inc(sqrt_ok, 1)
                act.wait_ge(lru_ok, f + 2)
                A(sqb, yb, ACT.Square).then_inc(sqb_ok, 1)

            act.wait_ge(sa_s, 1 + 8 + 1)
            A(saS[0:8, :], saS[0:8, :], ACT.Exp)
            A(sa_es[0:8, :], sa_mx[0:8, :], ACT.Exp, bias=sinkc[:, :], scale=-1.0).then_inc(sa_e, 1)
            act.wait_ge(sa_m, 2)
            A(saP[:, 0:NFT * NDEC], saT.rearrange("q a b -> q (a b)"), ACT.Square).then_inc(sa_sq, 1)

            def step3(t, p, rounds):
                act.wait_ge(x2_ok, 2 * t + 2)
                act.wait_ge(ss2_ok, t + 1)
                A(junk[:, :], x2_all[:, ds(t, 1), :].rearrange("q o c -> q (o c)"), ACT.Square,
                  accum_out=ss2[:, ds(t, 1)]).then_inc(ss2_ok, 1)
                act.wait_ge(xT2_ps, 2 * t + 1)
                A(xT2[:, 0:4, :], PS[:, 4, :].rearrange("q (a c) -> q a c", a=4), ACT.Copy).then_inc(xT2a_ok, 1)
                act.wait_ge(lgx_ok, t + 1)
                A(eg, lg[:, 0:4], ACT.Exp, bias=sc[:, 0:1], accum_out=sc[:, 1:2]).then_inc(ege_ok, 1)
                act.wait_ge(top_ok, t + 1)
                A(sc[:, 3:4], toe[:, 1:2], ACT.Exp, bias=sc[:, 2:3]).then_inc(eexp_ok, 1)
            with act.Fori(0, NT) as t:
                step3(t, 0, 0)

            def unit_x(n, p):
                act.wait_ge(xgT_ps, 2 * n + 1)
                A(xgT[:, p, 0:4, :], PS[:, 0, :].rearrange("q (a c) -> q a c", a=4), ACT.Copy).then_inc(xga_ok, 1)

            def unit_h(n, p):
                act.wait_ge(gu_ps, n + 1)
                A(hh[:, p, :], PS[:, 2 + p, 0:D_EXPERT], ACT.Tanh, scale=0.5).then_inc(th2_ok, 1)
                act.wait_ge(hT_ps, n + 1)
                A(hT[:, p, :, :], PS[:, 4, 0:2 * P].rearrange("q (a c) -> q a c", a=2), ACT.Copy).then_inc(hTa_ok, 1)

            def unit_y(n, p, rounds):
                if not (isinstance(rounds, int) and rounds == 0):
                    act.wait_ge(yo_out[p], 16 * rounds)
                act.wait_ge(y_ps, 2 * n + 1)
                A(yo[:, p, 0:512], PS[:, 5, :], ACT.Copy).then_inc(yoa_ok, 1)

            act.wait_ge(cnt_ok, 1)
            unit_x(0, 0)
            unit_x(1, 1)
            unit_h(0, 0)
            def pair(j):
                unit_x(2 * j + 2, 0)
                unit_y(2 * j, 0, j)
                unit_h(2 * j + 1, 1)
                unit_x(2 * j + 3, 1)
                unit_y(2 * j + 1, 1, j)
                unit_h(2 * j + 2, 0)
            pair(0)
            with act.Fori(1, NE // 2 - 1) as j:
                pair(j)
            unit_y(NE - 2, 0, NE // 2 - 1)
            unit_h(NE - 1, 1)
            unit_y(NE - 1, 1, NE // 2 - 1)
            act.wait_ge(vtab_ok, 1)
            nv = act.value_load(vtab[0:1, 2 * MAXV:2 * MAXV + 1], min_val=0, max_val=MAXV)
            with act.If(nv > 0):
                with act.Fori(0, nv) as v:
                    unit_x(v + NE, 0)
                    unit_h(v + NE, 0)
                    unit_y(v + NE, 0, v + NE // 2)
                act.wait_ge(vtab_ok, 1)
            with act.Fori(0, NT) as t:
                act.wait_ge(x3_ok, t + 1)
                act.wait_ge(ss3_ok, t + 1)
                A(junk[:, :], x2_all[:, ds(t, 1), :].rearrange("q o c -> q (o c)"), ACT.Square,
                  accum_out=ss3[:, ds(t, 1)]).then_inc(ss3_ok, 1)

        @block.vector
        def _(dve):
            V = nc.vector
            for first_pass in (lru_ok, xl_ok, y_ok):
                dve.sem_inc(first_pass, 1)
            dq = Count()

            def bc(ap, n):
                return ap.rearrange("q (m o) -> q m o", o=1).to_broadcast([P, ap.shape[-1], n])

            dve.wait_ge(par_in, 16 * 10)
            dve.wait_ge(cst_in, 16)
            dve.wait_ge(mem0, 7)
            lam = chp[:, :, C_LAM]
            e_, z_, q_ = drv[:, :, 0], drv[:, :, 1], drv[:, :, 2]
            V.tensor_scalar(z_, lam, -1.0, None, ALU.mult).then_inc(dve_done, dq.up())
            dve.wait_ge(dve_done, dq.now())
            V.tensor_tensor(e_, z_, lam, ALU.max).then_inc(expl_ok, 1)
            dve.wait_ge(drv_ok, 1)
            V.tensor_scalar(z_, e_, 2.0, None, ALU.add).then_inc(dve_done, dq.up())
            dve.wait_ge(dve_done, dq.now())
            V.reciprocal(z_, z_).then_inc(dve_done, dq.up())
            dve.wait_ge(dve_done, dq.now())
            V.tensor_tensor(z_, z_, e_, ALU.mult).then_inc(dve_done, dq.up())
            dve.wait_ge(dve_done, dq.now())
            V.tensor_tensor(e_, z_, z_, ALU.mult).then_inc(dve_done, dq.up())
            dve.wait_ge(dve_done, dq.now())
            V.tensor_scalar(q_, e_, 1.0 / 17, 1.0 / 15, ALU.mult, ALU.add).then_inc(dve_done, dq.up())
            dve.wait_ge(dve_done, dq.now())
            for n in (13, 11, 9, 7, 5, 3, 1):
                V.tensor_tensor(q_, q_, e_, ALU.mult).then_inc(dve_done, dq.up())
                dve.wait_ge(dve_done, dq.now())
                V.tensor_scalar(q_, q_, 1.0 / n, None, ALU.add).then_inc(dve_done, dq.up())
                dve.wait_ge(dve_done, dq.now())
            V.tensor_tensor(q_, q_, z_, ALU.mult).then_inc(dve_done, dq.up())
            dve.wait_ge(dve_done, dq.now())
            V.tensor_scalar(z_, lam, -2.0, 0.0, ALU.mult, ALU.max).then_inc(dve_done, dq.up())
            dve.wait_ge(dve_done, dq.now())
            V.scalar_tensor_tensor(q_, q_, 4.0, z_, ALU.mult, ALU.add).then_inc(dve_done, dq.up())
            dve.wait_ge(dve_done, dq.now())
            V.tensor_scalar(drv[:, :, 0], chp[:, :, C_BA], 0.5, None, ALU.mult).then_inc(dve_done, dq.up())
            V.tensor_scalar(drv[:, :, 1], chp[:, :, C_BX], 0.5, None, ALU.mult).then_inc(dve_done, dq.up())
            dve.wait_ge(dve_done, dq.now())

            def step1(t, p, att, mask):
                b = t - 1
                dve.wait_ge(x_sq, t + 1)
                V.tensor_scalar(varx[:, ds(t, 1)], ssx[:, ds(t, 1)], 1.0 / D_MODEL, EPS, ALU.mult, ALU.add)\
                    .then_inc(x_var, 1)
                if att:
                    for q in range(4):
                        dve.wait_ge(s_ps, 4 * b + q + 1)
                        if q == 0:
                            dve.wait_ge(pt_ps, 4 * b + 1)
                        V.scalar_tensor_tensor(E[:, q, :], PS[:, q, :], HEAD_DIM ** -0.5, mask, ALU.mult, ALU.add).then_inc(dve_done, dq.up())
                        dve.wait_ge(dve_done, dq.now())
                        V.reduce_max(mx[:, 2 * q:2 * q + 2], E[:, q, :].rearrange("q (a c) -> q a c", a=2), AX_X).then_inc(dve_done, dq.up())
                    dve.wait_ge(dve_done, dq.now())
                    V.tensor_tensor(mx, mx, sinkb[:, :], ALU.max).then_inc(dve_done, dq.up())
                    dve.wait_ge(dve_done, dq.now())
                    V.tensor_tensor(dsink, sinkb[:, :], mx, ALU.subtract)
                    V.tensor_scalar(nm, mx, -1.0, None, ALU.mult).then_inc(nmax_ok, 1)
                    for q in (1, 3):
                        dve.wait_ge(pt_ps, 4 * b + q + 2)
                        V.tensor_copy(PT[:, q, :], PS[:, q, :]).then_inc(ptd_ok, 1)
                    dve.wait_ge(es_ok, b + 1)
                    dve.wait_ge(exp_ok, 8 * b + 8)
                    V.tensor_tensor(den, rs, es, ALU.add).then_inc(dve_done, dq.up())
                    dve.wait_ge(dve_done, dq.now())
                    V.reciprocal(rinv, den).then_inc(dve_done, dq.up())
                dve.wait_ge(u_ok, t + 1)
                cos = cst[:, ds(t * 64 + K_CS, 32)].rearrange("q (o c) -> q o c", o=1).to_broadcast([P, 20, 32])
                sin = cst[:, ds(t * 64 + (K_CS + 32), 32)].rearrange("q (o c) -> q o c", o=1).to_broadcast([P, 20, 32])
                uv = u_sb.rearrange("q (h c) -> q h c", c=32)
                V.tensor_tensor(t1.rearrange("q (h c) -> q h c", c=32), uv, cos, ALU.mult).then_inc(dve_done, dq.up())
                V.tensor_tensor(t2.rearrange("q (h c) -> q h c", c=32), uv, sin, ALU.mult).then_inc(dve_done, dq.up())
                dve.wait_ge(dve_done, dq.now())
                a4 = t1.rearrange("q (h two c) -> q h two c", two=2, c=32)
                b4 = t2.rearrange("q (h two c) -> q h two c", two=2, c=32)
                r4 = rot[:, p, :].rearrange("q (h two c) -> q h two c", two=2, c=32)
                V.tensor_tensor(r4[:, :, 0, :], a4[:, :, 0, :], b4[:, :, 1, :], ALU.subtract)
                V.tensor_tensor(r4[:, :, 1, :], a4[:, :, 1, :], b4[:, :, 0, :], ALU.add).then_inc(rot_ok, 1)
                if att:
                    dve.wait_ge(o_ps, b + 1)
                    dve.wait_ge(aT_ps, b + 1)
                    dve.wait_ge(ssa_ok, b + 1)
                    V.tensor_tensor(at_st.rearrange("q (h c) -> q h c", c=64), PS[:, 6, :].rearrange("q (h c) -> q h c", c=64),
                                    bc(rinv, 64), ALU.mult).then_inc(attn_ok, 1)
                dve.wait_ge(qkT_ps, 2 * t + 2)
                V.tensor_copy(kT_all[:, ds(t * P + P, P)], PS[:, 5, 2 * P:3 * P]).then_inc(kT_ok, 1)

            step1(0, 0, False, None)
            N1 = 13
            d0 = dq.n
            with dve.Fori(0, 4) as j:
                dq.at(j * 2 * N1 + d0)
                step1(2 * j + 1, 1, True, cst[:, ds((j + 3) // 4 * 512 + K_MASK, 512)])
                assert dq.n == N1, dq.n
                dq.at(j * 2 * N1 + d0 + N1)
                step1(2 * j + 2, 0, True, cst[:, K_MASK + 512:K_MASK + 1024])
                assert dq.n == N1, dq.n
            dq.at(d0 + 8 * N1)

            dve.wait_ge(pt_ps, 4 * NPT + 1)
            dve.wait_ge(x_rstd, NT)
            dg = E.rearrange("q a c -> q (a c)")
            for t in range(NT):
                o = V.tensor_scalar(dg[:, t * P:(t + 1) * P], ident, rsx[:, t:t + 1], None, ALU.mult)
            o.then_inc(diag_ok, 1)
            dve.wait_ge(qz_ok, NT)
            dve.wait_ge(kT_ok, NT)
            V.tensor_copy(Qs, qz[:, 0, :, 0:NDEC].rearrange("q h b -> q b h"))
            V.tensor_copy(kTs[:, :, 0], kT_all[:, P + SEQ:P + SEQ + NDEC]).then_inc(sa_q, 1)
            dve.wait_ge(rbc_ps, 1)
            V.tensor_copy(rbc[:, 0:1024].rearrange("q (a c) -> q a c", a=2), PS[:, 0:2, :])
            V.tensor_copy(rbc[:, 1024:1024 + P], PS[:, 2, 0:P]).then_inc(rbc_ok, 1)
            dve.wait_ge(rbc_ok, 1)
            dve.wait_ge(aT_ps, NPT + 1)
            dve.wait_ge(ssa_ok, NPT + 1)
            dve.wait_ge(qkT_ps, 2 * NT)
            V.memset(xlb[:, 0:CONV - 1], 0.0).then_inc(dve_done, dq.up())
            dve.wait_ge(dve_done, dq.now())
            V.memset(mT_all[:, NFT:KD, TOKENS:], 0.0).then_inc(dve_done, dq.up())
            dve.wait_ge(dve_done, dq.now())

            N2 = 19
            base2 = dq.base + dq.n
            with dve.Fori(0, NFT) as f:
                dq.at(f * N2 + base2)
                dve.wait_ge(gate_ok, 6 * f + 1)
                dve.wait_ge(s_ok, f + 1)
                dve.wait_ge(lru_ok, f + 1)
                V.tensor_copy(cp, chp[:, ds(f, 1), :].rearrange("q o c -> q (o c)"))
                V.tensor_copy(dv, drv[:, ds(f, 1), :].rearrange("q o c -> q (o c)")).then_inc(cp_ok, 1)
                dve.wait_ge(cp_ok, f + 1)
                for c in range(3):
                    dve.wait_ge(xl_ps, 3 * f + c + 1)
                    V.tensor_tensor(xlb[:, CONV - 1 + c * CHUNK:CONV - 1 + (c + 1) * CHUNK], PS[:, c, 0:CHUNK],
                                    rbc[:, c * CHUNK:(c + 1) * CHUNK], ALU.mult).then_inc(xl_ok, 1)
                dve.wait_ge(xl_ok, 3 * f + 4)
                for j in range(CONV):
                    wj = cp[:, C_W + j:C_W + j + 1]
                    dst, src = cT[:, 0:SEQ], xlb[:, j:j + SEQ]
                    dds = cT[:, SEQ:TOKENS]
                    srs = cp[:, C_ST + 8 * j:C_ST + 8 * j + 8] if j < CONV - 1 else xlb[:, CONV - 1 + SEQ:CONV - 1 + TOKENS]
                    if j == 0:
                        V.tensor_scalar(dst, src, wj, cp[:, C_B:C_B + 1], ALU.mult, ALU.add).then_inc(dve_done, dq.up())
                        V.tensor_scalar(dds, srs, wj, cp[:, C_B:C_B + 1], ALU.mult, ALU.add).then_inc(dve_done, dq.up())
                        dve.wait_ge(dve_done, dq.now())
                    else:
                        V.scalar_tensor_tensor(dst, src, wj, dst, ALU.mult, ALU.add).then_inc(dve_done, dq.up())
                        V.scalar_tensor_tensor(dds, srs, wj, dds, ALU.mult, ALU.add).then_inc(dve_done, dq.up())
                        dve.wait_ge(dve_done, dq.now())
                V.tensor_copy(smo[:, ds(f, 1), O_XL:O_XL + 3], xlb[:, SEQ:SEQ + 3].rearrange("q (o c) -> q o c", o=1))
                V.tensor_copy(smo[:, ds(f, 1), O_XS:O_XS + 8], xlb[:, CONV - 1 + SEQ:].rearrange("q (o c) -> q o c", o=1))\
                    .then_inc(conv_ok, 1)
                for c in range(3):
                    dve.wait_ge(yg_ps, 3 * f + c + 1)
                    if c == 0:
                        dve.wait_ge(sqb_ok, f + 1)
                    V.tensor_tensor(yb[:, c * CHUNK:(c + 1) * CHUNK], PS[:, 3 + c, 0:CHUNK],
                                    rbc[:, c * CHUNK:(c + 1) * CHUNK], ALU.mult).then_inc(y_ok, 1)
                dve.wait_ge(gate_ok, 6 * f + 6 + 1)
                V.scalar_tensor_tensor(tib, tib, 1.0, cT, ALU.add, ALU.mult).then_inc(dve_done, dq.up())
                dve.wait_ge(s_ok, f + 2)
                V.tensor_scalar(wv, trs, 1.0, None, ALU.add).then_inc(dve_done, dq.up())
                dve.wait_ge(dve_done, dq.now())
                V.reciprocal(wv, wv).then_inc(dve_done, dq.up())
                dve.wait_ge(dve_done, dq.now())
                V.tensor_tensor(tib, tib, wv, ALU.mult).then_inc(dve_done, dq.up())
                dve.wait_ge(dve_done, dq.now())
                V.tensor_scalar(wv, wv, 2.0, -1.0, ALU.mult, ALU.add).then_inc(dve_done, dq.up())
                dve.wait_ge(sqrt_ok, f + 1)
                V.tensor_tensor(tib, tib, sqh, ALU.mult).then_inc(dve_done, dq.up())
                dve.wait_ge(dve_done, dq.now())
                V.tensor_tensor_scan(sqh[:, 0:SEQ], wv[:, 0:SEQ], tib[:, 0:SEQ], 0.0, ALU.mult, ALU.add).then_inc(dve_done, dq.up())
                V.tensor_tensor(sm8[:, 0, :], wv[:, SEQ:], cp[:, C_H0:C_H0 + 8], ALU.mult).then_inc(dve_done, dq.up())
                dve.wait_ge(dve_done, dq.now())
                V.tensor_tensor(sqh[:, SEQ:], sm8[:, 0, :], tib[:, SEQ:], ALU.add).then_inc(dve_done, dq.up())
                dve.wait_ge(dve_done, dq.now())
                V.tensor_copy(smo[:, ds(f, 1), O_HS:O_HS + 8], sqh[:, SEQ:].rearrange("q (o c) -> q o c", o=1))
                V.tensor_copy(smo[:, ds(f, 1), O_HL:O_HL + 1], sqh[:, SEQ - 1:SEQ].rearrange("q (o c) -> q o c", o=1))
                dve.wait_ge(th_ok, f + 1)
                V.scalar_tensor_tensor(inn, inn, 1.0, yb, ALU.add, ALU.mult).then_inc(dve_done, dq.up())
                dve.wait_ge(dve_done, dq.now())
                V.scalar_tensor_tensor(yb, inn, 0.5, sqh, ALU.mult, ALU.mult).then_inc(dve_done, dq.up())
                dve.wait_ge(dve_done, dq.now())
                V.tensor_scalar(mT_all[:, ds(f + NFT, 1), 0:TOKENS].rearrange("q o c -> q (o c)"), yb,
                                cp[:, C_GN:C_GN + 1], None, ALU.mult).then_inc(lru_ok, 1)
                assert dq.n == N2, dq.n
            dq.at(base2 + NFT * N2)

            dve.wait_ge(sqb_ok, NFT + 1)
            dve.wait_ge(sqacc_ok, 1)
            dve.wait_ge(sa_s, 8)
            V.tensor_scalar(saS[0:8, :].rearrange("q (a c) -> q a c", a=2), PS[0:8, 0:2, :], HEAD_DIM ** -0.5, None,
                                    ALU.mult).then_inc(dve_done, dq.up())
            dve.wait_ge(dve_done, dq.now())
            s3 = saS[0:8, :].rearrange("q (b c) -> q b c", b=NDEC)
            V.reduce_max(sa_mx[0:8, :], s3, AX_X).then_inc(dve_done, dq.up())
            dve.wait_ge(dve_done, dq.now())
            V.tensor_scalar(sa_mx[0:8, :], sa_mx[0:8, :], sinkc[:, :], None, ALU.max).then_inc(sa_s, 1)
            dve.wait_ge(sa_s, 9)

            def bc8(ap):
                return ap.rearrange("q (m o) -> q m o", o=1).to_broadcast([8, NDEC, P])
            V.tensor_tensor(s3, s3, bc8(sa_mx[0:8, :]), ALU.subtract).then_inc(sa_s, 1)
            dve.wait_ge(sa_e, 1)
            V.reduce_sum(sa_sum[0:8, :], s3, AX_X).then_inc(dve_done, dq.up())
            dve.wait_ge(dve_done, dq.now())
            V.tensor_tensor(sa_sum[0:8, :], sa_sum[0:8, :], sa_es[0:8, :], ALU.add).then_inc(dve_done, dq.up())
            dve.wait_ge(dve_done, dq.now())
            V.reciprocal(sa_sum[0:8, :], sa_sum[0:8, :]).then_inc(dve_done, dq.up())
            dve.wait_ge(dve_done, dq.now())
            V.tensor_tensor(s3, s3, bc8(sa_sum[0:8, :]), ALU.mult).then_inc(sa_n, 1)
            dve.wait_ge(sa_pt, NDEC)
            V.tensor_copy(saP, PS[:, 2, 0:NDEC * N_HEADS]).then_inc(sa_pte, 1)
            dve.wait_ge(sa_pv, NDEC)
            for lo in range(2):
                half = slice(64 * lo, 64 * lo + 64)
                V.tensor_copy(saT[half], PS[half, 3, 0:64].rearrange("q (b t two) -> q t b two", two=2, b=NDEC)[:, :, :, lo]).then_inc(dve_done, dq.up())
            dve.wait_ge(dve_done, dq.now())
            for lo in range(2):
                half = slice(64 * lo, 64 * lo + 64)
                V.tensor_tensor(mT_all[half, 0:NFT, SEQ:TOKENS], saT[half],
                                gna[half, :].rearrange("q (m o) -> q m o", o=1).to_broadcast([64, NFT, NDEC]), ALU.mult)\
                    .then_inc(sa_m, 1)
            dve.wait_ge(ss_ps, 1)
            V.tensor_copy(ssl[:, 0:NPT], PS[:, 4, 0:NPT]).then_inc(dve_done, dq.up())
            V.tensor_copy(ssl[0:8, NPT:NT], PS[0:8, 4, NPT:NT]).then_inc(dve_done, dq.up())
            V.tensor_copy(ssa[0:8, NPT:NT], PS[0:8, 4, 16:17]).then_inc(dve_done, dq.up())
            dve.wait_ge(dve_done, dq.now())
            V.tensor_scalar(val, ssa, 1.0 / ATTN, EPS, ALU.mult, ALU.add)
            V.tensor_scalar(val2[:, 0, :], ssl, 1.0 / LRU, EPS, ALU.mult, ALU.add).then_inc(varal_ok, 1)
            V.memset(cnt, 0.0).then_inc(dve_done, dq.up())
            dve.wait_ge(dve_done, dq.now())
            V.memset(lg, -3e38).then_inc(dve_done, dq.up())
            dve.wait_ge(dve_done, dq.now())
            dve.wait_ge(ral_ok, 2)
            dve.wait_ge(pre_in, 16)

            def x2_half(t, p, n, rounds):
                if n == 0:
                    dve.wait_ge(x_in2[p], 16 * rounds)
                cols = slice(512 * n, 512 * n + 512)
                dve.wait_ge(op_ps, 2 * t + n + 1)
                if not isinstance(t, int) or t > 0 or n > 0:
                    dve.wait_ge(x2_ok, 2 * t + n)
                V.scalar_tensor_tensor(x2t, PS[:, 2 * n, :], ral[:, ds(t, 1)], xin[:, p, cols], ALU.mult, ALU.add).then_inc(dve_done, dq.up())
                dve.wait_ge(dve_done, dq.now())
                V.scalar_tensor_tensor(x2_all[:, ds(t, 1), cols].rearrange("q o c -> q (o c)"), PS[:, 2 * n + 1, :],
                                       val2[:, 1, ds(t, 1)], x2t, ALU.mult, ALU.add).then_inc(x2_ok, 1)

            def norm2(t, p, rounds):
                dve.wait_ge(ss2_ok, t + 2)
                V.tensor_scalar(var2[:, ds(t, 1)], ss2[:, ds(t, 1)], 1.0 / D_MODEL, EPS, ALU.mult, ALU.add)\
                    .then_inc(var2_ok, 1)
                dve.wait_ge(rs2_ok, t + 1)
                if not (isinstance(rounds, int) and rounds == 0):
                    dve.wait_ge(xt_out[p], 16 * rounds)
                V.scalar_tensor_tensor(xn[:, p, :], x2_all[:, ds(t, 1), :].rearrange("q o c -> q (o c)"), rs2[:, ds(t, 1)],
                                       g2b, ALU.mult, ALU.mult).then_inc(xn_ok, 1)

            def route(t):
                dve.wait_ge(xT2_ps, 2 * t + 2)
                V.tensor_copy(xT2[:, 4:8, :], PS[:, 5, :].rearrange("q (a c) -> q a c", a=4)).then_inc(xT2d_ok, 1)
                dve.wait_ge(r_ps, t + 1)
                if not isinstance(t, int) or t > 0:
                    dve.wait_ge(idx_ok, t)
                V.tensor_tensor(lg[:, 0:4], PS[:, 6, 0:4], brb[:, 0:4], ALU.add).then_inc(dve_done, dq.up())
                V.tensor_tensor(le, PS[:, 6, 4:NR], brb[:, 4:NR], ALU.add).then_inc(dve_done, dq.up())
                dve.wait_ge(dve_done, dq.now())
                alone(dve)
                V.max(top, lg).then_inc(dve_done, dq.up())
                dve.wait_ge(dve_done, dq.now())
                alone(dve)
                V.max_index(idxg[:, :], top, lg).then_inc(dve_done, dq.up())
                V.tensor_scalar(sc[:, 0:1], top[:, 0:1], -1.0, None, ALU.mult).then_inc(lgx_ok, 1)
                dve.wait_ge(dve_done, dq.now())
                V.tensor_copy(sc[:, 4:5], idxg[:, 0:1]).then_inc(dve_done, dq.up())
                dve.wait_ge(dve_done, dq.now())
                V.tensor_scalar(ohg, cst[:, K_IE:K_IE + 4], sc[:, 4:5], None, ALU.is_equal).then_inc(dve_done, dq.up())
                dve.wait_ge(dve_done, dq.now())
                V.tensor_tensor(lem, le.rearrange("q (g e) -> q e g", g=N_GROUPS),
                                        ohg.rearrange("q (o g) -> q o g", o=1).to_broadcast([P, N_PER_GROUP, N_GROUPS]), ALU.mult).then_inc(dve_done, dq.up())
                dve.wait_ge(dve_done, dq.now())
                V.reduce_sum(les, lem, AX_X).then_inc(dve_done, dq.up())
                dve.wait_ge(dve_done, dq.now())
                alone(dve)
                V.max(toe, les).then_inc(dve_done, dq.up())
                dve.wait_ge(dve_done, dq.now())
                alone(dve)
                V.max_index(idxp[:, :], toe, les).then_inc(dve_done, dq.up())
                V.tensor_scalar(sc[:, 2:3], toe[:, 0:1], -1.0, None, ALU.mult).then_inc(top_ok, 1)
                dve.wait_ge(dve_done, dq.now())
                V.tensor_copy(rr[:, 0, :], idxp[:, 0:2]).then_inc(dve_done, dq.up())
                dve.wait_ge(dve_done, dq.now())
                V.tensor_scalar(sc[:, 4:5], sc[:, 4:5], float(N_PER_GROUP), None, ALU.mult).then_inc(dve_done, dq.up())
                dve.wait_ge(dve_done, dq.now())
                V.tensor_scalar(rr[:, 0, :], rr[:, 0, :], sc[:, 4:5], None, ALU.add).then_inc(dve_done, dq.up())
                dve.wait_ge(dve_done, dq.now())
                for k in range(TOPK):
                    V.tensor_scalar(oh[:, k, :], cst[:, K_IE:K_IE + NE], rr[:, 0, k:k + 1], None, ALU.is_equal).then_inc(dve_done, dq.up())
                dve.wait_ge(dve_done, dq.now())
                V.tensor_tensor(M, oh[:, 0, :], oh[:, 1, :], ALU.add).then_inc(dve_done, dq.up())
                dve.wait_ge(dve_done, dq.now())
                V.tensor_scalar(M, M, cst[:, ds(t + K_VALID, 1)], None, ALU.mult).then_inc(M_ok, 1)
                dve.wait_ge(ege_ok, t + 1)
                dve.wait_ge(eexp_ok, t + 1)
                V.tensor_scalar(sc[:, 6:7], sc[:, 3:4], 1.0, None, ALU.add).then_inc(dve_done, dq.up())
                dve.wait_ge(dve_done, dq.now())
                V.tensor_tensor(sc[:, 6:7], sc[:, 6:7], sc[:, 1:2], ALU.mult).then_inc(dve_done, dq.up())
                dve.wait_ge(dve_done, dq.now())
                V.reciprocal(sc[:, 7:8], sc[:, 6:7]).then_inc(dve_done, dq.up())
                dve.wait_ge(dve_done, dq.now())
                V.tensor_copy(comb[:, ds(t, 1), 0:1], sc[:, 7:8].rearrange("q (o c) -> q o c", o=1)).then_inc(dve_done, dq.up())
                V.tensor_tensor(comb[:, ds(t, 1), 1:2], sc[:, 7:8].rearrange("q (o c) -> q o c", o=1),
                                sc[:, 3:4].rearrange("q (o c) -> q o c", o=1), ALU.mult).then_inc(dve_done, dq.up())
                dve.wait_ge(rk_ps, t + 1)
                V.tensor_tensor(rk, PS[:, 7, 0:NE], cnt, ALU.add).then_inc(dve_done, dq.up())
                V.tensor_tensor(cnt, PS[:, 7, NE:2 * NE], cnt, ALU.add).then_inc(dve_done, dq.up())
                dve.wait_ge(dve_done, dq.now())
                V.tensor_tensor(jnk32, oh, rk.rearrange("q (o c) -> q o c", o=1).to_broadcast([P, TOPK, NE]), ALU.mult).then_inc(dve_done, dq.up())
                dve.wait_ge(dve_done, dq.now())
                V.reduce_sum(rr[:, 1, :], jnk32, AX_X).then_inc(dve_done, dq.up())
                dve.wait_ge(dve_done, dq.now())
                V.tensor_tensor(thrq, cst[:, K_THR:K_THR + 8].rearrange("q (o c) -> q o c", o=1)
                                        .to_broadcast([P, TOPK, 8]), bc(rr[:, 1, :], 8), ALU.is_le).then_inc(dve_done, dq.up())
                dve.wait_ge(dve_done, dq.now())
                V.reduce_sum(rr[:, 2, :], thrq, AX_X).then_inc(dve_done, dq.up())
                dve.wait_ge(dve_done, dq.now())
                row = NE * MAXC
                V.tensor_scalar(rr[:, 3, :], rr[:, 0, :], float(MAXC), None, ALU.mult).then_inc(dve_done, dq.up())
                dve.wait_ge(dve_done, dq.now())
                V.scalar_tensor_tensor(rr[:, 3, :], rr[:, 2, :], float(1 - CAP * row), rr[:, 3, :], ALU.mult, ALU.add).then_inc(dve_done, dq.up())
                dve.wait_ge(dve_done, dq.now())

            def place(t, p, rounds):
                if not (isinstance(rounds, int) and rounds == 0):
                    dve.wait_ge(scat[p], 32 * rounds)
                V.scalar_tensor_tensor(idxs[:, p, :], rr[:, 1, :], float(NE * MAXC), rr[:, 3, :], ALU.mult, ALU.add)\
                    .then_inc(idx_ok, 1)

            N3 = 31
            x2_half(0, 0, 0, 1)
            base3 = dq.base + dq.n
            dq.at(base3)

            def step3(t, p, rounds):
                x2_half(t, p, 1, None)
                norm2(t, p, rounds[0])
                if rounds[1] is not None:
                    x2_half(t + 1, 1 - p, 0, rounds[1])
                route(t)
                place(t, p, rounds[0])

            step3(0, 0, (0, 1))
            assert dq.n == N3, dq.n
            dq.at(base3 + N3)
            step3(1, 1, (0, 2))
            with dve.Fori(0, 3) as j:
                dq.at(j * 2 * N3 + base3 + 2 * N3)
                step3(2 * j + 2, 0, (j + 1, j + 2))
                dq.at(j * 2 * N3 + base3 + 3 * N3)
                step3(2 * j + 3, 1, (j + 1, j + 3))
            dq.at(base3 + 8 * N3)
            step3(8, 0, (4, None))
            V.tensor_tensor(bigc, bc(cnt, 8), cst[:, K_THR:K_THR + 8].rearrange("q (o c) -> q o c", o=1)
                                    .to_broadcast([P, NE, 8]), ALU.is_gt).then_inc(dve_done, dq.up())
            dve.wait_ge(dve_done, dq.now())
            V.reduce_sum(xe, bigc, AX_X).then_inc(dve_done, dq.up())
            dve.wait_ge(dve_done, dq.now())
            V.tensor_tensor_scan(incl, ones[:, 0:NE], xe, 0.0, ALU.mult, ALU.add).then_inc(dve_done, dq.up())
            dve.wait_ge(dve_done, dq.now())
            V.tensor_tensor(lev, incl.rearrange("q (o c) -> q o c", o=1).to_broadcast([P, MAXV, NE]),
                                    bc(cst[:, K_IV:K_IV + MAXV], NE), ALU.is_le).then_inc(dve_done, dq.up())
            dve.wait_ge(dve_done, dq.now())
            V.tensor_tensor(lex, lev, xe.rearrange("q (o c) -> q o c", o=1).to_broadcast([P, MAXV, NE]), ALU.mult).then_inc(dve_done, dq.up())
            V.reduce_sum(ev[:, 0, :], lev, AX_X).then_inc(dve_done, dq.up())
            dve.wait_ge(dve_done, dq.now())
            V.reduce_sum(ev[:, 1, :], lex, AX_X).then_inc(dve_done, dq.up())
            dve.wait_ge(dve_done, dq.now())
            V.tensor_tensor(ev[:, 1, :], cst[:, K_IV:K_IV + MAXV], ev[:, 1, :], ALU.subtract).then_inc(dve_done, dq.up())
            dve.wait_ge(dve_done, dq.now())
            V.scalar_tensor_tensor(ev[:, 1, :], ev[:, 0, :], float(MAXC), ev[:, 1, :], ALU.mult, ALU.add).then_inc(dve_done, dq.up())
            dve.wait_ge(dve_done, dq.now())
            V.tensor_scalar(ev[:, 1, :], ev[:, 1, :], 1.0, None, ALU.add).then_inc(dve_done, dq.up())
            dve.wait_ge(dve_done, dq.now())
            V.tensor_copy(vtab[:, 0:2 * MAXV], ev[0:1].rearrange("q a c -> q (a c)"))
            V.tensor_copy(vtab[:, 2 * MAXV:2 * MAXV + 1], incl[0:1, NE - 1:NE]).then_inc(vtab_ok, 1)
            dve.wait_ge(vtab_ok, 1)
            for p in range(2):
                dve.wait_ge(xt_out[p], 16 * (5 - p))
            dve.wait_ge(op_ps, 2 * NT)
            V.memset(thrq, 0.0).then_inc(cnt_ok, 1)

            def unit_x(n, p):
                dve.wait_ge(xgT_ps, 2 * n + 2)
                V.tensor_copy(xgT[:, p, 4:8, :], PS[:, 1, :].rearrange("q (a c) -> q a c", a=4)).then_inc(xgd_ok, 1)

            def unit_h(n, p):
                dve.wait_ge(th2_ok, n + 1)
                V.scalar_tensor_tensor(hh[:, p, :], hh[:, p, :], 1.0, PS[:, 2 + p, 0:D_EXPERT], ALU.add, ALU.mult).then_inc(dve_done, dq.up())
                dve.wait_ge(dve_done, dq.now())
                V.scalar_tensor_tensor(hh[:, p, :], hh[:, p, :], 0.5, PS[:, 2 + p, D_EXPERT:2 * D_EXPERT], ALU.mult, ALU.mult)\
                    .then_inc(h_ok, 1)

            def unit_y(n, p, rounds):
                if not (isinstance(rounds, int) and rounds == 0):
                    dve.wait_ge(yo_out[p], 16 * rounds)
                dve.wait_ge(y_ps, 2 * n + 2)
                V.tensor_copy(yo[:, p, 512:1024], PS[:, 6, :]).then_inc(yod_ok, 1)

            base4 = dq.base + dq.n
            dq.at(base4)
            unit_x(0, 0)
            unit_x(1, 1)
            unit_h(0, 0)
            def pair(j):
                dq.at(2 * j + base4 + 1)
                unit_x(2 * j + 2, 0)
                unit_y(2 * j, 0, j)
                unit_h(2 * j + 1, 1)
                unit_x(2 * j + 3, 1)
                unit_y(2 * j + 1, 1, j)
                unit_h(2 * j + 2, 0)
            pair(0)
            with dve.Fori(1, NE // 2 - 1) as j:
                pair(j)
            dq.at(base4 + NE - 1)
            unit_y(NE - 2, 0, NE // 2 - 1)
            unit_h(NE - 1, 1)
            unit_y(NE - 1, 1, NE // 2 - 1)
            nv = dve.value_load(vtab[0:1, 2 * MAXV:2 * MAXV + 1], min_val=0, max_val=MAXV)
            with dve.If(nv > 0):
                with dve.Fori(0, nv) as v:
                    dq.at(v + base4 + NE)
                    unit_x(v + NE, 0)
                    unit_h(v + NE, 0)
                    unit_y(v + NE, 0, v + NE // 2)
                dve.wait_ge(vtab_ok, 1)

            def add_y(t, p, rounds, base):
                dve.wait_ge(yp_in[p], 16 * rounds)
                x2 = x2_all[:, ds(t, 1), :].rearrange("q o c -> q (o c)")
                V.scalar_tensor_tensor(x2, yp[:, p, 0:D_MODEL], comb[:, ds(t, 1), 0:1].rearrange("q o c -> q (o c)"), x2,
                                       ALU.mult, ALU.add).then_inc(x3a, 1)
                dve.wait_ge(x3a, t + 1)
                V.scalar_tensor_tensor(x2, yp[:, p, D_MODEL:], comb[:, ds(t, 1), 1:2].rearrange("q o c -> q (o c)"), x2,
                                       ALU.mult, ALU.add).then_inc(x3_ok, 1)

            def finish(t, p, rounds):
                dve.wait_ge(ss3_ok, t + 2)
                V.tensor_scalar(ss3[:, ds(t, 1)], ss3[:, ds(t, 1)], 1.0 / D_MODEL, EPS, ALU.mult, ALU.add)\
                    .then_inc(var3_ok, 1)
                dve.wait_ge(rs3_ok, t + 1)
                if not (isinstance(rounds, int) and rounds == 0):
                    dve.wait_ge(o_out[p], 16 * rounds)
                V.scalar_tensor_tensor(ob[:, p, :], x2_all[:, ds(t, 1), :].rearrange("q o c -> q (o c)"), rs3[:, ds(t, 1)],
                                       gfb, ALU.mult, ALU.mult).then_inc(ob_ok, 1)

            dve.wait_ge(gf_in, 16)
            add_y(0, 0, 1, 0)
            add_y(1, 1, 1, 0)
            finish(0, 0, 0)
            add_y(2, 0, 2, 0)
            finish(1, 1, 0)
            with dve.Fori(0, 3) as j:
                add_y(2 * j + 3, 1, j + 2, 0)
                finish(2 * j + 2, 0, j + 1)
                add_y(2 * j + 4, 0, j + 3, 0)
                finish(2 * j + 3, 1, j + 1)
            finish(8, 0, 4)

        @block.tensor
        def _(pe):
            MM, TR = nc.tensor.matmul, nc.tensor.transpose
            for first_pass in (pt_ps, aT_ps):
                pe.sem_inc(first_pass, 1)

            def step1(t, p, rounds, att):
                b = t - 1
                pe.wait_ge(x_in[p], 16 * rounds)
                for k in range(KD):
                    o = TR(PS[:, 2 + k // 4, (k % 4) * P:(k % 4 + 1) * P], xin[:, p, k * P:(k + 1) * P], ident)
                    if k % 4 == 3:
                        o.then_inc(xT_ps, 1)
                if att:
                    pe.wait_ge(qz_ok, t)
                    pe.wait_ge(kT_ok, t)
                    for q in range(4):
                        if q >= 2:
                            pe.wait_ge(xs_ok, 2 * t + q - 1)
                        for h in range(2):
                            o = MM(PS[:, q, 256 * h:256 * h + 256], qz[:, 1 - p, 2 * q + h, :], kT_all[:, ds(b * P, 2 * P)],
                                   start=True, stop=True)
                        o.then_inc(s_ps, 1)
                else:
                    pe.wait_ge(wqkv_in, 16)
                pe.wait_ge(xs_ok, 2 * t + 2)
                for k in range(KD):
                    MM(PS[:, 4, :], xs[:, p, k, :], wqkv[:, k, 0:ATTN], start=(k == 0), stop=(k == KD - 1))
                    o = MM(PS[:, 5, 0:2 * KV], xs[:, p, k, :], wqkv[:, k, ATTN:QKV], start=(k == 0), stop=(k == KD - 1))
                o.then_inc(qkv_ps, 1)
                if att:
                    for q in range(4):
                        pe.wait_ge(exp_ok, 8 * b + 2 * q + 2)
                        for c in range(4):
                            o = TR(PS[:, q, c * P:(c + 1) * P], E[:, q, c * P:(c + 1) * P], ident)
                        o.then_inc(pt_ps, 1)
                    pe.wait_ge(aT_ok, b + 1)
                    pe.wait_ge(v_ok, t)
                    for q in range(4):
                        pe.wait_ge(ptd_ok if q % 2 else pta_ok, 2 * b + q // 2 + 1)
                        for h in range(2):
                            for kk in range(2):
                                o = MM(PS[:, 6, q * P + 64 * h:q * P + 64 * h + 64], PT[:, q, (2 * h + kk) * P:(2 * h + kk + 1) * P],
                                       v_all[:, ds(b + kk, 1), 64 * h:64 * h + 64].rearrange("q o c -> q (o c)"),
                                       start=(kk == 0), stop=(kk == 1))
                    o.then_inc(o_ps, 1)
                pe.wait_ge(rot_ok, t + 1)
                pe.wait_ge(v_ok, t + 1)
                for k in range(4):
                    o = TR(PS[:, 7, k * P:(k + 1) * P], rot[:, p, k * P:(k + 1) * P], ident)
                o.then_inc(qkT_ps, 1)
                TR(PS[:, 5, 2 * P:3 * P], rot[:, p, ATTN:], ident).then_inc(qkT_ps, 1)
                if att:
                    pe.wait_ge(attn_ok, b + 1)
                    for k in range(4):
                        o = TR(PS[:, 6, k * P:(k + 1) * P], at_st[:, k * P:(k + 1) * P], ident)
                    o.then_inc(aT_ps, 1)

            pe.wait_ge(cst_in, 16)
            pe.wait_ge(mem0, 7)
            step1(0, 0, 1, False)
            with pe.Fori(0, 4) as j:
                step1(2 * j + 1, 1, j + 1, True)
                step1(2 * j + 2, 0, j + 2, True)

            pe.wait_ge(diag_ok, 1)
            dg = E.rearrange("q a c -> q (a c)")
            MM(PS[:, 0, :], ones[:, :], dg[:, 0:512], start=True, stop=True)
            MM(PS[:, 1, :], ones[:, :], dg[:, 512:1024], start=True, stop=True)
            MM(PS[:, 2, 0:P], ones[:, :], dg[:, 1024:1024 + P], start=True, stop=True).then_inc(rbc_ps, 1)
            pe.wait_ge(rbc_ok, 1)
            pe.wait_ge(aT_ok, NPT + 1)
            pe.wait_ge(xTall_ok, NT + 1)

            with pe.Fori(0, NFT // 2) as j:
                for p in range(2):
                    f = 2 * j + p
                    pe.wait_ge(wxy_in[p], 32 * j + 32)
                    pe.wait_ge(xl_ok, 3 * f + 1)
                    for k in range(KD):
                        for c in range(3):
                            o = MM(PS[:, c, 0:CHUNK], wxy[p][:, k, 0:P], xT_all[:, k, c * CHUNK:(c + 1) * CHUNK],
                                   start=(k == 0), stop=(k == KD - 1))
                            if k == KD - 1:
                                o.then_inc(xl_ps, 1)
                    pe.wait_ge(y_ok, 3 * f + 1)
                    for k in range(KD):
                        for c in range(3):
                            o = MM(PS[:, 3 + c, 0:CHUNK], wxy[p][:, k, P:2 * P], xT_all[:, k, c * CHUNK:(c + 1) * CHUNK],
                                   start=(k == 0), stop=(k == KD - 1))
                            if k == KD - 1:
                                o.then_inc(yg_ps, 1)
                    pe.wait_ge(conv_ok, f + 1)
                    for c in range(3):
                        for g in range(2):
                            if c == 0 and g == 0:
                                pe.wait_ge(gate_ok, 6 * f + 1)
                            elif c > 0:
                                pe.wait_ge(gate_ok, 6 * f + 2 * (c - 1) + g + 2)
                            MM(PS[:, 6 + g, 0:CHUNK], wgate[:, p, g * P:(g + 1) * P], cT[:, c * CHUNK:(c + 1) * CHUNK],
                               start=True, stop=True).then_inc(gt_ps, 1)

            pe.wait_ge(sa_q, 1)
            pe.wait_ge(vnew_in, 16)
            pe.wait_ge(xl_ok, 3 * NFT + 1)
            for b in range(NDEC):
                MM(PS[0:8, b // 4, (b % 4) * P:(b % 4 + 1) * P], Qs[:, b, :], kTs[:, b, :], start=True, stop=True)\
                    .then_inc(sa_s, 1)
            pe.wait_ge(sa_n, 1)
            for b in range(NDEC):
                MM(PS[:, 2, 8 * b:8 * b + 8], saS[0:8, b * P:(b + 1) * P], ident[0:8, 0:8], start=True, stop=True)\
                    .then_inc(sa_pt, 1)
            pe.wait_ge(sa_pte, 1)
            pe.wait_ge(y_ok, 3 * NFT + 1)
            for b in range(NDEC):
                MM(PS[:, 3, 8 * b:8 * b + 8], Vs[:, b, :], saP[:, 8 * b:8 * b + 8], start=True, stop=True)\
                    .then_inc(sa_pv, 1)
            pe.wait_ge(sqacc_ok, 1)
            for t in range(NT):
                rows = P if t < NPT else NDEC
                MM(PS[0:rows, 4, t:t + 1], sqacc[:, t * P:t * P + rows], ones[:, 0:1], start=True, stop=True)
            pe.wait_ge(sa_sq, 1)
            for k in range(NFT):
                o = MM(PS[0:NDEC, 4, 16:17], saP[:, 8 * k:8 * k + 8], ones[:, 0:1], start=(k == 0), stop=(k == NFT - 1))
            o.then_inc(ss_ps, 1)

            pe.wait_ge(wout_in, 16)
            pe.wait_ge(varal_ok, 1)

            def op_half(t, p, n):
                if n == 0:
                    pe.wait_ge(mts_ok, t + 1)
                if not isinstance(t, int) or t > 0:
                    pe.wait_ge(x2_ok, 2 * t - 1 + n)
                for g in range(2):
                    for k in range(4):
                        o = MM(PS[:, 2 * n + g, :], mTs[:, p, 4 * g + k, :], wout[:, 4 * g + k, 512 * n:512 * n + 512],
                               start=(k == 0), stop=(k == 3))
                o.then_inc(op_ps, 1)

            def xT2_(t, p):
                pe.wait_ge(xn_ok, t + 1)
                for k in range(KD):
                    o = TR(PS[:, 4 + k // 4, (k % 4) * P:(k % 4 + 1) * P], xn[:, p, k * P:(k + 1) * P], ident)
                    if k % 4 == 3:
                        o.then_inc(xT2_ps, 1)

            def router(t):
                pe.wait_ge(xT2a_ok, t + 1)
                pe.wait_ge(xT2d_ok, t + 1)
                for k in range(KD):
                    o = MM(PS[:, 6, 0:NR], xT2[:, k, :], wr[:, k, :], start=(k == 0), stop=(k == KD - 1))
                o.then_inc(r_ps, 1)

            def ranks(t):
                pe.wait_ge(M_ok, t + 1)
                MM(PS[:, 7, 0:NE], upper, M, start=True, stop=True)
                MM(PS[:, 7, NE:2 * NE], ones[:, :], M, start=True, stop=True).then_inc(rk_ps, 1)

            def step3(t, p):
                op_half(t + 1, 1 - p, 0)
                xT2_(t, p)
                router(t)
                op_half(t + 1, 1 - p, 1)
                ranks(t)
            op_half(0, 0, 0)
            op_half(0, 0, 1)
            with pe.Fori(0, 4) as j:
                step3(2 * j, 0)
                step3(2 * j + 1, 1)
            xT2_(8, 0)
            router(8)
            ranks(8)

            pe.wait_ge(cnt_ok, 1)

            def unit_x(n, p, rounds):
                pe.wait_ge(xg_in[p], 16 * rounds)
                if not (isinstance(n, int) and n == 0):
                    pe.wait_ge(xga_ok, n)
                    pe.wait_ge(xgd_ok, n)
                for k in range(KD):
                    o = TR(PS[:, k // 4, (k % 4) * P:(k % 4 + 1) * P], xg[:, p, k * P:(k + 1) * P], ident)
                    if k % 4 == 3:
                        o.then_inc(xgT_ps, 1)

            def unit_gu(n, p, rounds):
                pe.wait_ge(xga_ok, n + 1)
                pe.wait_ge(xgd_ok, n + 1)
                pe.wait_ge(wexp_in[p], 16 * rounds)
                for k in range(KD):
                    o = MM(PS[:, 2 + p, :], xgT[:, p, k, :], wexp[p][:, k * 512:(k + 1) * 512], start=(k == 0), stop=(k == KD - 1))
                o.then_inc(gu_ps, 1)

            def unit_hT(n, p):
                pe.wait_ge(h_ok, n + 1)
                for k in range(KF):
                    o = TR(PS[:, 4, k * P:(k + 1) * P], hh[:, p, k * P:(k + 1) * P], ident)
                o.then_inc(hT_ps, 1)

            def unit_y(n, p):
                pe.wait_ge(hTa_ok, n + 1)
                if not (isinstance(n, int) and n == 0):
                    pe.wait_ge(yoa_ok, n)
                    pe.wait_ge(yod_ok, n)
                for half in range(2):
                    for k in range(KF):
                        o = MM(PS[:, 5 + half, :], hT[:, p, k, :],
                               wexp[p][:, KD * 512 + k * D_MODEL + half * 512:KD * 512 + k * D_MODEL + half * 512 + 512],
                               start=(k == 0), stop=(k == KF - 1))
                    o.then_inc(y_ps, 1)

            unit_x(0, 0, 1)
            unit_gu(0, 0, 1)
            unit_x(1, 1, 1)
            unit_hT(0, 0)
            with pe.Fori(0, NE // 2 - 1) as j:
                unit_gu(2 * j + 1, 1, j + 1)
                unit_x(2 * j + 2, 0, j + 2)
                unit_y(2 * j, 0)
                unit_hT(2 * j + 1, 1)
                unit_gu(2 * j + 2, 0, j + 2)
                unit_x(2 * j + 3, 1, j + 2)
                unit_y(2 * j + 1, 1)
                unit_hT(2 * j + 2, 0)
            unit_gu(NE - 1, 1, NE // 2)
            unit_y(NE - 2, 0)
            unit_hT(NE - 1, 1)
            unit_y(NE - 1, 1)
            pe.wait_ge(vtab_ok, 1)
            nv = pe.value_load(vtab[0:1, 2 * MAXV:2 * MAXV + 1], min_val=0, max_val=MAXV)
            with pe.If(nv > 0):
                with pe.Fori(0, nv) as v:
                    unit_x(v + NE, 0, v + NE // 2 + 1)
                    unit_gu(v + NE, 0, v + NE // 2 + 1)
                    unit_hT(v + NE, 0)
                    unit_y(v + NE, 0)
                pe.wait_ge(vtab_ok, 1)


def constants():
    c = np.zeros((P, K_N), np.float32)
    c[:, K_ID:K_ID + P] = np.eye(P)
    c[:, K_UP:K_UP + P] = np.triu(np.ones((P, P)), 1)
    r, k = np.arange(P)[:, None], np.arange(2 * P)[None, :]
    seen = (k > r) & (k <= r + P)
    for kind, ok in enumerate((seen & (k >= P), seen)):
        m = np.where(ok, 0.0, MASKED)
        c[:, K_MASK + 512 * kind:K_MASK + 512 * (kind + 1)] = np.concatenate([m, m], 1)
    inv = 10000.0 ** (-2.0 * np.arange(32) / HEAD_DIM)
    for t in range(NT):
        pos = t * P + np.arange(P) if t < NPT else np.full(P, PAST_LEN)
        ang = pos.astype(np.float32)[:, None] * inv.astype(np.float32)[None, :]
        c[:, K_CS + 64 * t:K_CS + 64 * t + 32] = np.cos(ang)
        c[:, K_CS + 64 * t + 32:K_CS + 64 * t + 64] = np.sin(ang)
    c[:, K_THR:K_THR + 8] = CAP * np.arange(1, 9)
    c[:, K_IE:K_IE + NE] = np.arange(NE)
    c[:, K_IV:K_IV + MAXV] = np.arange(MAXV)
    c[:, K_VALID:K_VALID + NT] = 1.0
    c[NDEC:, K_VALID + NPT] = 0.0
    tok = (np.arange(NT)[None, :] * P + np.arange(P)[:, None]).astype(np.int32)
    pay = np.stack([tok, 2 * tok, tok, 2 * tok + 1], -1).astype(np.int32)
    return c, pay


def layout(inputs):
    n = {k: np.asarray(v) for k, v in inputs.items()}
    pair = [0, 4, 1, 5, 2, 6, 3, 7]
    cst, pay = constants()
    w_in = n["w_in"][0]
    q = w_in[:, :ATTN].reshape(D_MODEL, N_HEADS, HEAD_DIM)[:, pair].reshape(D_MODEL, ATTN)
    wqkv = np.concatenate([q, w_in[:, ATTN:QKV]], 1)

    def tiles(m):
        return np.ascontiguousarray(m.reshape(-1, P, m.shape[1]).transpose(1, 0, 2))

    xl, yg = w_in[:, QKV:QKV + LRU], w_in[:, QKV + LRU:]
    wxy = np.stack([tiles(np.concatenate([xl[:, f * P:(f + 1) * P], yg[:, f * P:(f + 1) * P]], 1)) for f in range(NFT)])
    wg = np.zeros((NFT, P, 2 * P), np.float32)
    for g, name in enumerate(("w_rg_a", "w_rg_x")):
        for h in range(N_HEADS):
            f, o = h // 2, 64 * (h % 2)
            wg[f, o:o + 64, g * P + o:g * P + o + 64] = n[name][0, h]

    def chan(v):
        return v.reshape(NFT, P, -1).transpose(1, 0, 2)
    chp = np.concatenate([
        chan(n["w_conv"][0].T), chan(n["b_conv"][0]), chan(n["b_rg_a"][0]), chan(n["b_rg_x"][0]), chan(n["lru_lambda"][0]),
        chan(n["gn_lru"][0]), chan(n["state_conv"][0].transpose(2, 1, 0).reshape(LRU, 24)), chan(n["state_lru_h"][0].T)], 2)
    gna = n["gn_attn"][0].reshape(N_HEADS, HEAD_DIM)[pair].reshape(NFT, P).T
    wo = n["w_out"][0]
    woa = wo[:ATTN].reshape(N_HEADS, HEAD_DIM, D_MODEL)[pair].reshape(ATTN, D_MODEL)
    wgu = np.concatenate([n["w_exp_gate"][0], n["w_exp_up"][0]], -1).reshape(NE, KD, P, 2 * D_EXPERT)
    wd = n["w_exp_down"][0].reshape(NE, KF, P, D_MODEL)
    wexp = np.concatenate([wgu.transpose(0, 2, 1, 3).reshape(NE, P, -1), wd.transpose(0, 2, 1, 3).reshape(NE, P, -1)], 2)
    ck, cv = n["cache_k_win"][0], n["cache_v_win"][0]
    out = {
        "x": np.concatenate([n["x_prompt"][0], n["x_sample"][:, 0]], 0),
        "cst": cst, "payload": pay, "g1": n["ln1_g"][0].reshape(KD, P).T, "gna": gna,
        "sinkc": n["attn_sinks"][0][pair][:, None], "sinks": n["attn_sinks"][0][pair], "chp": chp,
        "wr": tiles(np.concatenate([n["w_router_grp"][0], n["w_router_exp"][0]], 1)),
        "kTs": ck.reshape(NDEC, WINDOW, KV).transpose(2, 0, 1), "Vs": cv.reshape(NDEC, WINDOW, KV).transpose(1, 0, 2),
        "b_router": np.concatenate([n["b_router_grp"][0], n["b_router_exp"][0]]),
        "g2": n["ln2_g"][0], "gf": n["final_g"], "wqkv": tiles(wqkv), "wxy": wxy, "wgate": wg,
        "wout": tiles(np.concatenate([woa, wo[ATTN:]], 0)), "wexp": wexp,
        "conv_old": n["state_conv"][0], "cache_k": ck.reshape(NDEC, WINDOW, KV), "cache_v": cv.reshape(NDEC, WINDOW, KV),
    }
    return {k: np.ascontiguousarray(v) for k, v in out.items()}


OUTS = {"y": (TOKENS, D_MODEL), "p_k": (WINDOW, KV), "p_v": (WINDOW, KV), "s_k": (NDEC, WINDOW, KV),
        "s_v": (NDEC, WINDOW, KV), "s_c": (NDEC, CONV - 2, LRU), "rec": (P, NFT, O_N)}


def kernel(**inputs):
    import concourse.bacc as bacc
    from concourse.bass_utils import run_bass_kernel_spmd as run

    arrays = layout(inputs)
    nc = bacc.Bacc("TRN2", target_bir_lowering=False, num_devices=1)
    aps = {k: nc.dram_tensor("in_" + k, v.shape, mybir.dt.from_np(v.dtype), kind="ExternalInput").ap() for k, v in arrays.items()}
    aps.update({k: nc.dram_tensor("out_" + k, s, F32, kind="ExternalOutput").ap() for k, s in OUTS.items()})
    build(nc, aps)
    r = run(nc, [{"in_" + k: v for k, v in arrays.items()}], core_ids=[0]).results[0]
    y, rec = r["out_y"], r["out_rec"]

    def rows(lo, hi):
        return rec[:, :, lo:hi].transpose(2, 1, 0).reshape(hi - lo, LRU)
    xs, hs, xlast, hlast = rows(O_XS, O_HS), rows(O_HS, O_XL), rows(O_XL, O_HL), rows(O_HL, O_N)
    s_conv = np.concatenate([r["out_s_c"], xs[:, None]], 1)[None]
    win = (1, 1, WINDOW, N_KV, HEAD_DIM)
    swin = (1, NDEC, WINDOW, N_KV, HEAD_DIM)
    return (y[:SEQ].reshape(1, SEQ, D_MODEL), y[SEQ:].reshape(NDEC, 1, D_MODEL), r["out_p_k"].reshape(win),
            r["out_p_v"].reshape(win), xlast.reshape(1, 1, 3, LRU), hlast.reshape(1, 1, LRU),
            r["out_s_k"].reshape(swin), r["out_s_v"].reshape(swin), s_conv, hs.reshape(1, NDEC, LRU))
```

```python
from contextlib import ExitStack

import numpy as np

import concourse.bass as bass
from concourse import mybir

F32 = mybir.dt.float32
BF16 = mybir.dt.bfloat16
I32 = mybir.dt.int32
U32 = mybir.dt.uint32
ALU = mybir.AluOpType
ACT = mybir.ActivationFunctionType
AX_X = mybir.AxisListType.X
ds = bass.ds

P = 128
D_MODEL = 1024
KD = D_MODEL // P
SEQ = 1024
NDEC = 8
TOKENS = SEQ + NDEC
NPT = SEQ // P
NT = NPT + 1
HEAD_DIM = 64
N_HEADS = 8
N_KV = 2
WINDOW = 128
ATTN = N_HEADS * HEAD_DIM
KV = N_KV * HEAD_DIM
QKV = ATTN + 2 * KV
LRU = D_MODEL - ATTN
NFT = LRU // P
CONV = 4
CHUNK = TOKENS // 3
PAST_LEN = 2048
N_GROUPS = 4
N_PER_GROUP = 8
NE = N_GROUPS * N_PER_GROUP
NR = N_GROUPS + NE
D_EXPERT = D_MODEL // 4
KF = D_EXPERT // P
TOPK = 2
CAP = P
MAXC = -(-TOKENS // CAP)
MAXV = TOPK * TOKENS // CAP
EPS = 1e-6
MASKED = -1e30
NOROW = 1 << 20
GELU_C = 0.7978845608028654
GELU_A = 0.044715

C_W, C_B, C_BA, C_BX, C_LAM, C_GN, C_ST, C_H0 = 0, 4, 5, 6, 7, 8, 9, 33
C_N = 41
O_XS, O_HS, O_XL, O_HL, O_N = 0, 8, 16, 19, 20
K_ID, K_UP, K_MASK, K_CS, K_THR, K_IE, K_IV, K_VALID = 0, 128, 256, 1280, 1856, 1864, 1896, 1912
K_N = 1912 + NT


class Count:

    def __init__(self):
        self.base, self.n = 0, 0

    def up(self):
        self.n += 1
        return 1

    def now(self):
        return self.base + self.n

    def at(self, base):
        self.base, self.n = base, 0


def build(nc, a):
    xtab = nc.dram_tensor("xtab", (NT * P, D_MODEL), F32).ap()
    ypair = nc.dram_tensor("ypair", (TOPK * TOKENS, D_MODEL), F32).ap()
    rowlist = nc.dram_tensor("rowlist", (CAP * NE * MAXC, 2), I32).ap()
    vnew = nc.dram_tensor("vnew", (NDEC, KV), F32).ap()

    with ExitStack() as ctx:
        def sb(name, shape, dt=F32):
            return ctx.enter_context(nc.sbuf_tensor(name, shape, dt))

        def sem(name):
            return ctx.enter_context(nc.semaphore(name))

        class Region:

            def __init__(self, name, words):
                self.t, self.words, self.at = sb(name, [P, words]), words, 0

            def cut(self, *shape):
                n = int(np.prod(shape))
                v = self.t[:, self.at:self.at + n]
                self.at += n
                assert self.at <= self.words, (self.at, self.words)
                if len(shape) == 2:
                    v = v.rearrange("p (a b) -> p a b", a=shape[0])
                if len(shape) == 3:
                    v = v.rearrange("p (a b c) -> p a b c", a=shape[0], b=shape[1])
                return v

            def phase(self, at=0):
                self.at = at

        PS = ctx.enter_context(nc.psum_tensor("PS", [P, 8, 512], F32))

        cst = sb("cst", [P, K_N])
        ones = sb("ones", [P, P])
        mhalf = sb("mhalf", [P, 1])
        warm = sb("warm", [P, 1])
        g1 = sb("g1", [P, KD])
        gna = sb("gna", [P, NFT])
        sinkb = sb("sinkb", [P, N_HEADS])
        sinkc = sb("sinkc", [N_HEADS, 1])
        chp = sb("chp", [P, NFT, C_N])
        drv = sb("drv", [P, NFT, 4])
        wr = sb("wr", [P, KD, NR])
        brb = sb("brb", [P, NR])
        payload = sb("payload", [P, NT, 4], I32)
        stat = sb("stat", [P, 12, NT])
        ssx, varx, rsx, ssa, ssl, val, ral, ss2, var2, rs2 = (stat[:, i, :] for i in range(10))
        ss3, rs3 = stat[:, 10, :], stat[:, 11, :]
        val2 = sb("val2", [P, 2, NT])
        comb = sb("comb", [P, NT, 2])
        xin = sb("xin", [P, 2, D_MODEL])
        rot = sb("rot", [P, 2, ATTN + KV])
        smo = sb("smo", [P, NFT, O_N])
        ident = cst[:, K_ID:K_ID + P]
        upper = cst[:, K_UP:K_UP + P]

        RA = Region("RA", KD * NT * P)
        xT_all = RA.cut(KD, NT * P)
        RA.phase()
        x2_all = RA.cut(NT, D_MODEL)

        RB = Region("RB", KD * NT * P)
        mT_all = RB.cut(KD, NT * P)
        RB.phase(NFT * NT * P)
        PT = RB.cut(4, 512)
        t1 = RB.cut(ATTN + KV)
        t2 = RB.cut(ATTN + KV)

        WXP = KD * D_EXPERT * 2 + KF * D_MODEL
        RC = Region("RC", KD * D_MODEL)
        wqkv = RC.cut(KD, QKV)
        wxy1 = RC.cut(KD, 2 * P)
        RC.phase()
        wout = RC.cut(KD, D_MODEL)
        KQ = KD * QKV // D_MODEL
        RC.phase()
        wexp1 = RC.cut(WXP)

        RE = Region("RE", 9900)
        wxy0 = RE.cut(KD, 2 * P)
        wgate = RE.cut(2, 2 * P)
        v_all = RE.cut(NT + 1, KV)
        kT_all = RE.cut((NT + 1) * P)
        rbc = RE.cut(NT * P)
        kTs = RE.cut(NDEC, P)
        Vs = RE.cut(NDEC, P)
        Qs = RE.cut(NDEC, N_HEADS)
        cp = RE.cut(C_N)
        dv = RE.cut(4)
        RE.phase(RE.at - NDEC * (2 * P + N_HEADS) - C_N - 4)
        mTs = RE.cut(2, KD, P)
        RE.phase()
        wexp0 = RE.cut(WXP)
        wxy = [wxy0, wxy1]
        RB.phase()
        wexp2 = RB.cut(WXP)
        wexp = [wexp0, wexp1, wexp2]

        RD = Region("RD", 9240)
        E = RD.cut(4, 512)
        qz = RD.cut(2, N_HEADS, P)
        xs = RD.cut(2, KD, P)
        u_sb = RD.cut(ATTN + KV)
        at_st = RD.cut(ATTN)
        rs = RD.cut(N_HEADS)
        mx = RD.cut(N_HEADS)
        nm = RD.cut(N_HEADS)
        dsink = RD.cut(N_HEADS)
        es = RD.cut(N_HEADS)
        den = RD.cut(N_HEADS)
        rinv = RD.cut(N_HEADS)
        RD.phase()
        xlb = RD.cut(CONV - 1 + TOKENS)
        cT = RD.cut(TOKENS)
        yb = RD.cut(TOKENS)
        inn = RD.cut(TOKENS)
        trs = xlb[:, CONV - 1:]
        tib = RD.cut(TOKENS)
        wv = RD.cut(TOKENS)
        sqh = RD.cut(TOKENS)
        sqacc = RD.cut(TOKENS)
        sqb = inn
        sm8 = RD.cut(4, 8)
        sa_mx = RD.cut(8)
        sa_es = RD.cut(8)
        sa_sum = RD.cut(8)
        saS = xin[:, 0, :]
        saP = xin[:, 1, 0:NDEC * N_HEADS]
        saT = xin[:, 1, P:P + NFT * NDEC].rearrange("q (a b) -> q a b", a=NFT)
        RD.phase()
        xn = RD.cut(2, D_MODEL)
        xT2 = RD.cut(KD, P)
        g2b = RD.cut(D_MODEL)
        x2t = RD.cut(512)
        lg = RD.cut(8)
        le = RD.cut(NE)
        top = RD.cut(8)
        eg = RD.cut(4)
        ohg = RD.cut(4)
        lem = RD.cut(N_PER_GROUP, N_GROUPS)
        les = RD.cut(8)
        toe = RD.cut(8)
        sc = RD.cut(16)
        oh = RD.cut(2, NE)
        cnt = RD.cut(NE)
        M = RD.cut(NE)
        rk = RD.cut(NE)
        thrq = RD.cut(2, 8)
        rr = RD.cut(4, 2)
        jnk32 = RD.cut(2, NE)
        bigc = RD.cut(NE, 8)
        xe = RD.cut(NE)
        incl = RD.cut(NE)
        lev = RD.cut(MAXV, NE)
        lex = RD.cut(MAXV, NE)
        ev = RD.cut(2, MAXV)
        RD.phase()
        xg = RD.cut(3, D_MODEL)
        xgT = RD.cut(2, KD, P)
        hh = RD.cut(2, D_EXPERT)
        hT = RD.cut(2, KF, P)
        yo = RD.cut(2, D_MODEL)
        RD.phase()
        RB.phase()
        yp = RB.cut(4, TOPK * D_MODEL)
        RD.phase()
        ob = RD.cut(2, D_MODEL)
        RD.phase(RD.words - D_MODEL)
        gfb = RD.cut(D_MODEL)
        junk = sb("junk", [P, D_MODEL], BF16)
        idxg = sb("idxg", [P, 8], U32)
        idxp = sb("idxp", [P, 8], U32)
        idxs = sb("idxs", [P, 2, 2], U32)
        pays = sb("pays", [P, 2, 4], I32)
        lists = sb("lists", [P, NE * MAXC, 2], I32)
        pidg = sb("pidg", [P, 3, 1], I32)
        pids = sb("pids", [P, 2, 1], I32)
        vtab = sb("vtab", [1, 2 * MAXV + 2], I32)

        cst_in = sem("cst_in")
        par_in = sem("par_in")
        id_in = sem("id_in")
        g1_in = sem("g1_in")
        sinks_in = sem("sinks_in")
        wqkv_in = [sem("wqkv_in0"), sem("wqkv_in1")]
        mem0 = sem("mem0")
        x_sq = sem("x_sq")
        x_var = sem("x_var")
        x_rstd = sem("x_rstd")
        xT_ps = sem("xT_ps")
        xs_ok = sem("xs_ok")
        xTall_ok = sem("xTall_ok")
        s_ps = sem("s_ps")
        nmax_ok = sem("nmax_ok")
        exp_ok = sem("exp_ok")
        es_ok = sem("es_ok")
        qkv_ps = sem("qkv_ps")
        u_ok = sem("u_ok")
        v_ok = sem("v_ok")
        pt_ps = sem("pt_ps")
        pta_ok = sem("pta_ok")
        ptd_ok = sem("ptd_ok")
        o_ps = sem("o_ps")
        rot_ok = sem("rot_ok")
        qkT_ps = sem("qkT_ps")
        qz_ok = sem("qz_ok")
        kT_ok = sem("kT_ok")
        attn_ok = sem("attn_ok")
        aT_ps = sem("aT_ps")
        aT_ok = sem("aT_ok")
        ssa_ok = sem("ssa_ok")
        drv_ok = sem("drv_ok")
        expl_ok = sem("expl_ok")
        diag_ok = sem("diag_ok")
        rbc_ps = sem("rbc_ps")
        rbc_ok = sem("rbc_ok")
        xl_ps = sem("xl_ps")
        yg_ps = sem("yg_ps")
        gt_ps = sem("gt_ps")
        xl_ok = sem("xl_ok")
        conv_ok = sem("conv_ok")
        y_ok = sem("y_ok")
        gate_ok = sem("gate_ok")
        s_ok = sem("s_ok")
        a_ok = sem("a_ok")
        y2_ok = sem("y2_ok")
        inn_ok = sem("inn_ok")
        th_ok = sem("th_ok")
        sqrt_ok = sem("sqrt_ok")
        out_ok = sem("out_ok")
        lru_ok = sem("lru_ok")
        sqb_ok = sem("sqb_ok")
        sqacc_ok = sem("sqacc_ok")
        cp_ok = sem("cp_ok")
        pre_in = sem("pre_in")
        vnew_out = sem("vnew_out")
        vnew_in = sem("vnew_in")
        sa_q = sem("sa_q")
        sa_s = sem("sa_s")
        sa_e = sem("sa_e")
        sa_n = sem("sa_n")
        sa_pt = sem("sa_pt")
        sa_pte = sem("sa_pte")
        sa_pv = sem("sa_pv")
        sa_m = sem("sa_m")
        sa_sq = sem("sa_sq")
        ss_ps = sem("ss_ps")
        varal_ok = sem("varal_ok")
        ral_ok = sem("ral_ok")
        smo_out = sem("smo_out")
        kwin_out = sem("kwin_out")
        kv_dec = sem("kv_dec")
        wout_in = [sem("wout_in0"), sem("wout_in1")]
        op_ps = sem("op_ps")
        x2_ok = sem("x2_ok")
        ss2_ok = sem("ss2_ok")
        var2_ok = sem("var2_ok")
        rs2_ok = sem("rs2_ok")
        xn_ok = sem("xn_ok")
        xT2_ps = sem("xT2_ps")
        xT2a_ok = sem("xT2a_ok")
        xT2d_ok = sem("xT2d_ok")
        r_ps = sem("r_ps")
        lgx_ok = sem("lgx_ok")
        ege_ok = sem("ege_ok")
        top_ok = sem("top_ok")
        eexp_ok = sem("eexp_ok")
        M_ok = sem("M_ok")
        rk_ps = sem("rk_ps")
        idx_ok = sem("idx_ok")
        pay_ok = sem("pay_ok")
        lists_init = sem("lists_init")
        lists_in = sem("lists_in")
        mta_ok = sem("mta_ok")
        mts_ok = sem("mts_ok")
        cnt_ok = sem("cnt_ok")
        vtab_ok = sem("vtab_ok")
        passed = sem("passed")
        xgT_ps = sem("xgT_ps")
        xga_ok = sem("xga_ok")
        xgd_ok = sem("xgd_ok")
        gu_ps = sem("gu_ps")
        th2_ok = sem("th2_ok")
        h_ok = sem("h_ok")
        hg_ok = sem("hg_ok")
        hT_ps = sem("hT_ps")
        hTa_ok = sem("hTa_ok")
        y_ps = sem("y_ps")
        yoa_ok = sem("yoa_ok")
        yod_ok = sem("yod_ok")
        pidg_ok = sem("pidg_ok")
        pids_ok = sem("pids_ok")
        x3_ok = sem("x3_ok")
        ss3_ok = sem("ss3_ok")
        var3_ok = sem("var3_ok")
        rs3_ok = sem("rs3_ok")
        ob_ok = sem("ob_ok")
        gm0 = sem("gm0")
        dve_done = sem("dve_done")
        pool_done = sem("pool_done")
        g_free = sem("g_free")
        x3a = sem("x3a")
        gf_in = sem("gf_in")
        x_in = [sem("x_in0"), sem("x_in1")]
        x_in2 = [sem("x_in2_0"), sem("x_in2_1")]
        wxy_in = [sem("wxy_in0"), sem("wxy_in1")]
        xt_out = [sem("xt_out0"), sem("xt_out1")]
        scat = [sem("scat0"), sem("scat1")]
        wexp_in = [sem("wexp_in0"), sem("wexp_in1"), sem("wexp_in2")]
        xg_in = [sem("xg_in0"), sem("xg_in1"), sem("xg_in2")]
        yo_out = [sem("yo_out0"), sem("yo_out1")]
        yp_in = [sem("yp_in%d" % i) for i in range(4)]
        o_out = [sem("o_out0"), sem("o_out1")]

        block = ctx.enter_context(nc.Block())

        def unit(j, i):
            return 6 * j + i, i % 2, i % 3, 3 * j + i // 2, 2 * j + i // 3

        def further(v):
            return v + NE, 0, 0, v + len(range(0, NE, 2)), v + len(range(0, NE, 3))

        def alone(eng):
            eng.sem_inc(passed, 1)

        @block.sync
        def _(sp):
            def load_x(t, p, rows, sems):
                sp.dma_start(xin[0:rows, p, :], a["x"][ds(t * P, rows), :]).then_inc(sems[p], 16)

            load_x(0, 0, P, x_in)
            sp.dma_start(cst[:, 0:K_MASK], a["cst"][:, 0:K_MASK]).then_inc(id_in, 16)
            sp.dma_start(g1[:, :], a["g1"]).then_inc(g1_in, 16)
            sp.dma_start(wqkv[:, 0:KD // 2, :], a["wqkv"][:, 0:KD // 2, :]).then_inc(wqkv_in[0], 16)
            sp.dma_start(wqkv[:, KD // 2:, :], a["wqkv"][:, KD // 2:, :]).then_inc(wqkv_in[1], 16)
            sp.dma_start(cst[:, K_MASK:], a["cst"][:, K_MASK:]).then_inc(cst_in, 16)
            sp.dma_start(sinkb[:, :], a["sinks"].partition_broadcast(P)).then_inc(sinks_in, 16)
            load_x(1, 1, P, x_in)
            for dst, name in ((gna[:, :], "gna"), (sinkc[:, :], "sinkc"), (chp[:, :, :], "chp"),
                              (wr[:, :, :], "wr"), (payload[:, :, :], "payload"), (kTs, "kTs"), (Vs, "Vs")):
                sp.dma_start(dst, a[name]).then_inc(par_in, 16)
            sp.dma_start(brb[:, :], a["b_router"].partition_broadcast(P)).then_inc(par_in, 16)
            sp.dma_start(a["s_k"][:, 0:WINDOW - 1, :], a["cache_k"][:, 1:WINDOW, :]).then_inc(kv_dec, 16)
            sp.dma_start(a["s_v"][:, 0:WINDOW - 1, :], a["cache_v"][:, 1:WINDOW, :]).then_inc(kv_dec, 16)
            sp.dma_start(a["s_c"], a["conv_old"][:, 1:CONV - 1, :]).then_inc(kv_dec, 16)

            def reload_x(t, p, rows):
                sp.wait_ge(xT_ps, 2 * t - 2)
                alone(sp)
                sp.wait_ge(x_sq, t - 1)
                load_x(t, p, rows, x_in)

            with sp.Fori(0, 3) as j:
                reload_x(2 * j + 2, 0, P)
                reload_x(2 * j + 3, 1, P)
            reload_x(8, 0, NDEC)

            def load_wxy(f, p):
                sp.dma_start(wxy[p], a["wxy"][f]).then_inc(wxy_in[p], 16)
                sp.dma_start(wgate[:, p, :], a["wgate"][f]).then_inc(wxy_in[p], 16)
            for f in range(2):
                load_wxy(f, f)
            sp.wait_ge(rot_ok, NT)
            sp.wait_ge(v_ok, NT)
            sp.dma_start(a["p_k"], rot[:, 1, ATTN:]).then_inc(kwin_out, 16)
            sp.dma_start(a["p_v"], v_all[:, NPT, :]).then_inc(kwin_out, 16)
            sp.dma_start(a["s_k"][:, WINDOW - 1, :], rot[0:NDEC, 0, ATTN:]).then_inc(kwin_out, 16)
            sp.dma_start(a["s_v"][:, WINDOW - 1, :], v_all[0:NDEC, NT, :]).then_inc(kwin_out, 16)
            sp.dma_start(vnew, v_all[0:NDEC, NT, :]).then_inc(vnew_out, 16)
            sp.wait_ge(vnew_out, 16)
            sp.wait_ge(par_in, 16 * 8)
            sp.dma_start(Vs[0:1, :, :], vnew.rearrange("(o b) d -> o b d", o=1)).then_inc(vnew_in, 16)
            sp.wait_ge(qkv_ps, NT)
            sp.dma_start(wout[:, 0:KQ, :], a["wout"][:, 0:KQ, :]).then_inc(wout_in[0], 16)
            for p in range(2):
                sp.wait_ge(yg_ps, 3 * (p + 1))
                sp.wait_ge(gt_ps, 6 * (p + 1))
                if p == 0:
                    sp.wait_ge(wxy_in[0], 32)
                load_wxy(2 + p, p)
            sp.wait_ge(yg_ps, 3 * NFT)
            sp.dma_start(wout[:, KQ:, :], a["wout"][:, KQ:, :]).then_inc(wout_in[1], 16)
            sp.wait_ge(lru_ok, NFT + 1)
            sp.dma_start(a["rec"], smo[:, :, :]).then_inc(smo_out, 16)
            sp.wait_ge(aT_ps, NPT + 1)
            sp.wait_ge(ss_ps, 1)
            sp.dma_start(g2b, a["g2"].partition_broadcast(P)).then_inc(pre_in, 16)
            load_x(0, 0, P, x_in2)
            load_x(1, 1, P, x_in2)
            sp.dma_start(gfb, a["gf"].partition_broadcast(P)).then_inc(gf_in, 16)
            sp.wait_ge(sa_pv, NDEC)
            sp.wait_ge(vnew_out, 16)
            sp.wait_ge(kwin_out, 64)
            sp.dma_start(wexp[0], a["wexp"][0]).then_inc(wexp_in[0], 16)

            def step3(t, p, rows):
                sp.wait_ge(xn_ok, t + 1)
                sp.dma_start(xtab[ds(t * P, P), :], xn[:, p, :]).then_inc(xt_out[p], 16)
                if rows:
                    sp.wait_ge(x2_ok, 2 * t + 2)
                    load_x(t + 2, p, rows, x_in2)

            with sp.Fori(0, 3) as j:
                step3(2 * j, 0, P)
                step3(2 * j + 1, 1, P)
            step3(6, 0, NDEC)
            step3(7, 1, 0)
            step3(8, 0, 0)

            sp.wait_ge(op_ps, 2 * NT)
            sp.wait_ge(scat[1], 32 * (NPT // 2))
            sp.dma_start(wexp[1], a["wexp"][1]).then_inc(wexp_in[1], 16)
            sp.wait_ge(xg_in[0], 16)
            sp.dma_start(wexp[2], a["wexp"][2]).then_inc(wexp_in[2], 16)

            def load_expert(u):
                n, p2, p3, r2, r3 = u
                sp.wait_ge(y_ps, 2 * n - 4)
                sp.dma_start(wexp[p3], a["wexp"][ds(n, 1)].rearrange("o p n -> (o p) n")).then_inc(wexp_in[p3], 16)
            with sp.Fori(0, 4) as j:
                for i in range(6):
                    load_expert(unit(j, i + 3))
            for n in range(27, NE):
                load_expert(unit(0, n))
            sp.wait_ge(vtab_ok, 1)
            nv = sp.value_load(vtab[0:1, 2 * MAXV:2 * MAXV + 1], min_val=0, max_val=MAXV)
            with sp.If(nv > 0):
                with sp.Fori(0, nv) as v:
                    e = sp.value_load(vtab[0:1, ds(v, 1)], min_val=0, max_val=NE - 1)
                    sp.wait_ge(y_ps, 2 * v + 2 * NE)
                    sp.dma_start(wexp[0], a["wexp"][ds(e, 1)].rearrange("o p n -> (o p) n")).then_inc(wexp_in[0], 16)
                sp.wait_ge(vtab_ok, 1)
            sp.wait_ge(g_free, 1)

            def rows_of(t):
                return P if t < NPT else NDEC

            def load_y(t):
                rows = rows_of(t)
                sp.dma_start(yp[0:rows, t % 4, :], ypair[2 * t * P:2 * t * P + 2 * rows, :]
                             .rearrange("(q two) d -> q (two d)", two=2)).then_inc(yp_in[t % 4], 16)
            for t in range(4):
                load_y(t)
            for t in range(NT):
                if t + 4 < NT:
                    sp.wait_ge(x3_ok, t + 1)
                    load_y(t + 4)
                sp.wait_ge(ob_ok, t + 1)
                rows = rows_of(t)
                sp.dma_start(a["y"][t * P:t * P + rows, :], ob[0:rows, t % 2, :]).then_inc(o_out[t % 2], 16)
            sp.wait_ge(o_out[0], 16 * 5)
            sp.wait_ge(o_out[1], 16 * 4)
            sp.wait_ge(kwin_out, 64)
            sp.wait_ge(kv_dec, 48)
            sp.wait_ge(smo_out, 16)
            sp.wait_ge(vnew_in, 16)

        @block.gpsimd
        def _(pool):
            for first_pass in (xTall_ok,):
                pool.sem_inc(first_pass, 1)
            pool.memset(mhalf[:, :], -0.5).then_inc(mem0, 1)
            pool.memset(ones[:, :], 1.0).then_inc(mem0, 1)
            pool.memset(stat[:, :, :], 1.0).then_inc(mem0, 1)

            pool.memset(qz, 0.0).then_inc(mem0, 1)
            pool.memset(kT_all[:, 0:P], 0.0).then_inc(mem0, 1)
            pool.memset(v_all[:, 0, :], 0.0).then_inc(mem0, 1)
            pool.memset(mT_all[:, 0:NFT, SEQ:], 0.0).then_inc(mem0, 1)
            pool.memset(lists[:, :, :], NOROW).then_inc(gm0, 1)
            pool.wait_ge(gm0, 1)
            pool.dma_start(rowlist.rearrange("(p n) c -> p n c", p=CAP), lists[:, :, :]).then_inc(lists_init, 16)

            def root(out, var, signal):
                nc.gpsimd.tensor_tensor(out, var, mhalf[:, 0:1], ALU.pow).then_inc(signal, 1)

            pool.wait_ge(mem0, 7)
            def tile1(t, p):
                pool.wait_ge(xs_ok, 2 * t + 2)
                nc.gpsimd.tensor_copy(xT_all[:, :, ds(t * P, P)], xs[:, p]).then_inc(xTall_ok, 1)
                pool.wait_ge(x_var, t + 1)
                root(rsx[:, ds(t, 1)], varx[:, ds(t, 1)], x_rstd)
            tile1(0, 0)
            with pool.Fori(0, 4) as j:
                tile1(2 * j + 1, 1)
                tile1(2 * j + 2, 0)

            pool.wait_ge(aT_ps, NPT + 1)
            pool.wait_ge(qkT_ps, 2 * NT)
            pool.wait_ge(attn_ok, NPT)
            pool.wait_ge(ssa_ok, NPT + 1)
            pool.wait_ge(rbc_ps, 1)
            def stage(t, p, half=slice(0, KD)):
                return nc.gpsimd.tensor_copy(mTs[:, p, half], mT_all[:, half, ds(t * P, P)])

            def stage_next(t, p):
                pool.wait_ge(op_ps, 2 * t - 2)
                stage(t, p).then_inc(mts_ok, 1)

            pool.memset(sqacc, 0.0).then_inc(pool_done, 1)
            pool.wait_ge(aT_ok, NPT + 1)
            pool.wait_ge(sa_m, 2)
            for t in range(2):
                stage(t, t, slice(0, NFT)).then_inc(mta_ok, 1)
            with pool.Fori(0, NFT) as f:
                pool.wait_ge(y2_ok, f + 1)
                alone(pool)
                nc.gpsimd.tensor_scalar(inn, inn, GELU_A, 1.0, ALU.mult, ALU.add).then_inc(pool_done, 1)
                pool.wait_ge(pool_done, 2 * f + 2)
                nc.gpsimd.tensor_tensor(inn, inn, yb, ALU.mult).then_inc(inn_ok, 1)
                pool.wait_ge(sqb_ok, f + 2)
                nc.gpsimd.tensor_tensor(sqacc, sqacc, sqb, ALU.add).then_inc(pool_done, 1)
                pool.wait_ge(pool_done, 2 * f + 3)
            pool.memset(junk[:, 0:2], 0.0).then_inc(sqacc_ok, 1)
            pool.wait_ge(lru_ok, NFT + 1)
            for t in range(2):
                stage(t, t, slice(NFT, KD)).then_inc(mts_ok, 1)
            pool.wait_ge(varal_ok, 1)
            nc.gpsimd.tensor_tensor(ral, val, mhalf[:, 0:1].to_broadcast([P, NT]), ALU.pow).then_inc(ral_ok, 1)
            nc.gpsimd.tensor_tensor(val2[:, 1, :], val2[:, 0, :], mhalf[:, 0:1].to_broadcast([P, NT]), ALU.pow)\
              .then_inc(ral_ok, 1)


            def root2(t):
                pool.wait_ge(var2_ok, t + 1)
                root(rs2[:, ds(t, 1)], var2[:, ds(t, 1)], rs2_ok)

            def scatter(t, p, rows):
                pool.wait_ge(idx_ok, t + 1)
                nc.gpsimd.tensor_copy(pays[:, p, :], payload[:, ds(t, 1), :].rearrange("q o c -> q (o c)"))\
                  .then_inc(pay_ok, 1)
                pool.wait_ge(pay_ok, t + 1)
                alone(pool)
                for k in range(TOPK):
                    pool.indirect_dma_start(rowlist, bass.IndirectOffsetOnAxis(idxs[0:rows, p, k:k + 1], 0),
                                            pays[0:rows, p, 2 * k:2 * k + 2], None).then_inc(scat[p], 16)

            def scatter_done(p, rounds):
                pool.wait_ge(scat[p], 32 * rounds)

            pool.wait_ge(ss_ps, 1)
            pool.wait_ge(lru_ok, NFT + 1)
            pool.wait_ge(lists_init, 16)
            root2(0)
            with pool.Fori(0, 3) as j:
                stage_next(2 * j + 2, 0)
                root2(2 * j + 1)
                scatter(2 * j, 0, P)
                scatter_done(0, j + 1)
                stage_next(2 * j + 3, 1)
                root2(2 * j + 2)
                scatter(2 * j + 1, 1, P)
                scatter_done(1, j + 1)
            stage_next(8, 0)
            root2(7)
            scatter(6, 0, P)
            scatter_done(0, 4)
            root2(8)
            scatter(7, 1, P)
            scatter_done(1, 4)
            pool.wait_ge(r_ps, NT)
            for p in range(2):
                pool.wait_ge(xt_out[p], 16 * (5 - p))
            pool.memset(xg, 0.0).then_inc(gm0, 1)
            pool.wait_ge(gm0, 2)
            scatter(8, 0, NDEC)
            scatter_done(0, 5)
            pool.dma_start(lists[:, :, :], rowlist.rearrange("(p n) c -> p n c", p=CAP)).then_inc(lists_in, 16)
            pool.wait_ge(lists_in, 16)

            def gather(u, col):
                n, p2, p3, r2, r3 = u
                if not isinstance(n, int) or n >= 3:
                    pool.wait_ge(xgT_ps, 2 * n - 4)
                nc.gpsimd.tensor_copy(pidg[:, p3, :], lists[:, ds(col, 1), 0]).then_inc(pidg_ok, 1)
                pool.wait_ge(pidg_ok, n + 1)
                alone(pool)
                pool.indirect_dma_start(xg[:, p3, :], None, xtab,
                                        bass.IndirectOffsetOnAxis(pidg[:, p3, :].bitcast(U32), 0),
                                        bounds_check=TOKENS - 1, oob_is_err=False).then_inc(xg_in[p3], 16)

            def spread(u, col):
                n, p2, p3, r2, r3 = u
                if not isinstance(n, int) or n >= 2:
                    pool.wait_ge(yo_out[p2], 16 * r2)
                nc.gpsimd.tensor_copy(pids[:, p2, :], lists[:, ds(col, 1), 1]).then_inc(pids_ok, 1)
                pool.wait_ge(pids_ok, n + 1)
                pool.wait_ge(yoa_ok, n + 2)
                pool.wait_ge(yod_ok, n + 2)
                alone(pool)
                pool.indirect_dma_start(ypair, bass.IndirectOffsetOnAxis(pids[:, p2, :].bitcast(U32), 0),
                                        yo[:, p2, :], None,
                                        bounds_check=TOPK * TOKENS - 1, oob_is_err=False).then_inc(yo_out[p2], 16)

            for n in range(3):
                gather(unit(0, n), n * MAXC)

            def step4(j, i):
                gather(unit(j, i + 3), (6 * j + i + 3) * MAXC)
                spread(unit(j, i), (6 * j + i) * MAXC)
            for i in range(6):
                step4(0, i)
            with pool.Fori(1, 4) as j:
                for i in range(6):
                    step4(j, i)
            for n in range(24, NE):
                if n + 3 < NE:
                    gather(unit(0, n + 3), (n + 3) * MAXC)
                spread(unit(0, n), n * MAXC)
            for p in range(2):
                pool.wait_ge(yo_out[p], 16 * (NE // 2))
            pool.wait_ge(vtab_ok, 1)
            nv = pool.value_load(vtab[0:1, 2 * MAXV:2 * MAXV + 1], min_val=0, max_val=MAXV)
            with pool.If(nv > 0):
                with pool.Fori(0, nv) as v:
                    col = pool.value_load(vtab[0:1, ds(v + MAXV, 1)], min_val=0, max_val=NE * MAXC - 1)
                    pool.wait_ge(xgT_ps, 2 * v + 2 * NE)
                    gather(further(v), col)
                    spread(further(v), col)
                    pool.wait_ge(yo_out[0], 16 * v + 16 * (NE // 2 + 1))
                pool.wait_ge(vtab_ok, 1)
            pool.memset(junk[:, 0:2], 0.0).then_inc(g_free, 1)
            with pool.Fori(0, NT) as t:
                pool.wait_ge(var3_ok, t + 1)
                root(rs3[:, ds(t, 1)], ss3[:, ds(t, 1)], rs3_ok)

        @block.scalar
        def _(act):
            A = nc.scalar.activation
            for first_pass in (ssa_ok, aT_ok, gate_ok, s_ok, sqb_ok, ss2_ok, ss3_ok, yoa_ok):
                act.sem_inc(first_pass, 1)

            def step1(t, p, rounds, att):
                b = t - 1
                if att:
                    act.wait_ge(xTall_ok, t)
                for k in range(KD):
                    if k % 4 == 0:
                        act.wait_ge(xT_ps, 2 * t + 1 + k // 4)
                    o = A(xs[:, p, k, :], PS[:, 2 + k // 4, (k % 4) * P:(k % 4 + 1) * P], ACT.Copy, scale=g1[:, k:k + 1])
                    if k % 4 == 3:
                        o.then_inc(xs_ok, 1)
                act.wait_ge(x_in[p], 16 * rounds)
                if att:
                    act.wait_ge(x_sq, t)
                    act.wait_ge(ssa_ok, b + 1)
                A(junk[:, :], xin[:, p, :], ACT.Square, accum_out=ssx[:, ds(t, 1)]).then_inc(x_sq, 1)
                if att:
                    act.wait_ge(nmax_ok, b + 1)
                    for h in range(N_HEADS):
                        e = E[:, h // 2, (h % 2) * 256:(h % 2 + 1) * 256]
                        A(e, e, ACT.Exp, bias=nm[:, h:h + 1], accum_out=rs[:, h:h + 1]).then_inc(exp_ok, 1)
                    A(es, dsink, ACT.Exp).then_inc(es_ok, 1)
                    act.wait_ge(pt_ps, 4 * b + 2)
                    A(PT[:, 0, :], PS[:, 0, :], ACT.Copy).then_inc(pta_ok, 1)
                act.wait_ge(qkv_ps, t + 1)
                act.wait_ge(x_rstd, t + 1)
                if att:
                    act.wait_ge(rot_ok, t)
                A(u_sb[:, 0:ATTN], PS[:, 4, :], ACT.Copy, scale=rsx[:, ds(t, 1)])
                A(u_sb[:, ATTN:], PS[:, 5, 0:KV], ACT.Copy, scale=rsx[:, ds(t, 1)]).then_inc(u_ok, 1)
                A(v_all[:, ds(t + 1, 1), :], PS[:, 5, KV:2 * KV].rearrange("q (o c) -> q o c", o=1), ACT.Copy,
                  scale=rsx[:, ds(t, 1)]).then_inc(v_ok, 1)
                if att:
                    act.wait_ge(pt_ps, 4 * b + 4)
                    A(PT[:, 2, :], PS[:, 2, :], ACT.Copy).then_inc(pta_ok, 1)
                act.wait_ge(qkT_ps, 2 * t + 1)
                for lo in range(2):
                    half = slice(64 * lo, 64 * lo + 64)
                    o = A(qz[half, p, lo::2, :], PS[half, 7, :].rearrange("q (h c) -> q h c", h=4), ACT.Copy)
                o.then_inc(qz_ok, 1)
                if att:
                    act.wait_ge(attn_ok, b + 1)
                    act.wait_ge(x_sq, t + 1)
                    A(junk[:, 0:ATTN], at_st, ACT.Square, accum_out=ssa[:, ds(b, 1)]).then_inc(ssa_ok, 1)
                    act.wait_ge(aT_ps, b + 2)
                    for k in range(NFT):
                        o = A(mT_all[:, k, ds(b * P, P)], PS[:, 6, k * P:(k + 1) * P], ACT.Copy, scale=gna[:, k:k + 1])
                    o.then_inc(aT_ok, 1)

            act.wait_ge(g1_in, 16)
            act.wait_ge(mem0, 7)
            step1(0, 0, 1, False)
            act.wait_ge(par_in, 16 * 8)
            with act.Fori(0, 4) as j:
                step1(2 * j + 1, 1, j + 1, True)
                step1(2 * j + 2, 0, j + 2, True)

            act.wait_ge(sa_s, 1 + 8 + 1)
            A(saS[0:8, :], saS[0:8, :], ACT.Exp)
            A(sa_es[0:8, :], sa_mx[0:8, :], ACT.Exp, bias=sinkc[:, :], scale=-1.0).then_inc(sa_e, 1)
            act.wait_ge(expl_ok, 1)
            A(drv[:, :, 0], drv[:, :, 0], ACT.Exp, scale=-1.0).then_inc(drv_ok, 1)
            act.wait_ge(sa_m, 2)
            A(saP[:, 0:NFT * NDEC], saT.rearrange("q a b -> q (a b)"), ACT.Square).then_inc(sa_sq, 1)

            act.wait_ge(rbc_ok, 1)
            with act.Fori(0, NFT) as f:
                act.wait_ge(y_ok, 3 * f + 4)
                act.wait_ge(pool_done, 2 * f + 1)
                A(inn, yb, ACT.Square).then_inc(y2_ok, 1)
                for c in range(3):
                    cols = slice(c * CHUNK, (c + 1) * CHUNK)
                    act.wait_ge(gt_ps, 6 * f + 2 * c + 1)
                    if c == 0:
                        act.wait_ge(cp_ok, f + 1)
                    A(trs[:, cols], PS[:, 6, 0:CHUNK], ACT.Tanh, bias=dv[:, 0:1], scale=0.5).then_inc(gate_ok, 1)
                    act.wait_ge(gt_ps, 6 * f + 2 * c + 2)
                    A(tib[:, cols], PS[:, 7, 0:CHUNK], ACT.Tanh, bias=dv[:, 1:2], scale=0.5).then_inc(gate_ok, 1)
                act.wait_ge(gate_ok, 6 * f + 7)
                A(wv, trs, ACT.Exp, bias=dv[:, 3:4], scale=dv[:, 3:4]).then_inc(a_ok, 1)
                act.wait_ge(a_ok, f + 1)
                A(trs, trs, ACT.Tanh, bias=dv[:, 2:3], scale=dv[:, 2:3]).then_inc(s_ok, 1)
                act.wait_ge(inn_ok, f + 1)
                A(inn, inn, ACT.Tanh, scale=GELU_C).then_inc(th_ok, 1)
                act.wait_ge(s_ok, f + 2)
                A(sqh, trs, ACT.Sqrt, scale=0.25).then_inc(sqrt_ok, 1)
                act.wait_ge(out_ok, f + 1)
                A(sqb, yb, ACT.Square).then_inc(sqb_ok, 1)

            def step3(t):
                act.wait_ge(x2_ok, 2 * t + 2)
                act.wait_ge(ss2_ok, t + 1)
                A(junk[:, :], x2_all[:, ds(t, 1), :].rearrange("q o c -> q (o c)"), ACT.Square,
                  accum_out=ss2[:, ds(t, 1)]).then_inc(ss2_ok, 1)
                act.wait_ge(xT2_ps, 2 * t + 1)
                A(xT2[:, 0:4, :], PS[:, 4, :].rearrange("q (a c) -> q a c", a=4), ACT.Copy).then_inc(xT2a_ok, 1)
                act.wait_ge(lgx_ok, t + 1)
                A(eg, lg[:, 0:4], ACT.Exp, bias=sc[:, 0:1], accum_out=sc[:, 1:2]).then_inc(ege_ok, 1)
                act.wait_ge(top_ok, t + 1)
                A(sc[:, 3:4], toe[:, 1:2], ACT.Exp, bias=sc[:, 2:3]).then_inc(eexp_ok, 1)
            A(warm[:, :], mhalf[:, :], ACT.Exp)
            with act.Fori(0, NT) as t:
                step3(t)

            def unit_th(u):
                n, p2, p3, r2, r3 = u
                act.wait_ge(gu_ps, n + 1)
                A(hh[:, p2, :], PS[:, 2 + p2, 0:D_EXPERT], ACT.Tanh, scale=0.5).then_inc(th2_ok, 1)

            def unit_x(u):
                n, p2, p3, r2, r3 = u
                act.wait_ge(xgT_ps, 2 * n + 1)
                A(xgT[:, p2, 0:4, :], PS[:, 0, :].rearrange("q (a c) -> q a c", a=4), ACT.Copy).then_inc(xga_ok, 1)

            def unit_y(u):
                n, p2, p3, r2, r3 = u
                if not isinstance(n, int) or n >= 2:
                    act.wait_ge(yo_out[p2], 16 * r2)
                act.wait_ge(y_ps, 2 * n + 1)
                A(yo[:, p2, 0:512], PS[:, 5, :], ACT.Copy).then_inc(yoa_ok, 1)

            def unit_hT(u):
                n, p2, p3, r2, r3 = u
                act.wait_ge(hT_ps, n + 1)
                A(hT[:, p2, :, :], PS[:, 4, 0:2 * P].rearrange("q (a c) -> q a c", a=2), ACT.Copy).then_inc(hTa_ok, 1)

            act.wait_ge(cnt_ok, 1)
            unit_x(unit(0, 0))
            unit_th(unit(0, 0))
            unit_x(unit(0, 1))
            unit_hT(unit(0, 0))

            def step4(j, i, more):
                unit_th(unit(j, i + 1))
                if more:
                    unit_x(unit(j, i + 2))
                unit_y(unit(j, i))
                unit_hT(unit(j, i + 1))
            for i in range(6):
                step4(0, i, True)
            with act.Fori(1, 5) as j:
                for i in range(6):
                    step4(j, i, True)
            step4(5, 0, False)
            unit_y(unit(5, 1))
            act.wait_ge(vtab_ok, 1)
            nv = act.value_load(vtab[0:1, 2 * MAXV:2 * MAXV + 1], min_val=0, max_val=MAXV)
            with act.If(nv > 0):
                with act.Fori(0, nv) as v:
                    unit_x(further(v))
                    unit_th(further(v))
                    unit_hT(further(v))
                    unit_y(further(v))
                act.wait_ge(vtab_ok, 1)
            with act.Fori(0, NT) as t:
                act.wait_ge(x3_ok, t + 1)
                act.wait_ge(ss3_ok, t + 1)
                A(junk[:, :], x2_all[:, ds(t, 1), :].rearrange("q o c -> q (o c)"), ACT.Square,
                  accum_out=ss3[:, ds(t, 1)]).then_inc(ss3_ok, 1)

        @block.vector
        def _(dve):
            V = nc.vector
            for first_pass in (lru_ok, xl_ok, y_ok, yod_ok):
                dve.sem_inc(first_pass, 1)
            dq = Count()

            def bc(ap, n):
                return ap.rearrange("q (m o) -> q m o", o=1).to_broadcast([P, ap.shape[-1], n])

            dve.wait_ge(cst_in, 16)
            dve.wait_ge(sinks_in, 16)
            dve.wait_ge(mem0, 7)

            def step1(t, p, att, mask):
                b = t - 1
                dve.wait_ge(x_sq, t + 1)
                V.tensor_scalar(varx[:, ds(t, 1)], ssx[:, ds(t, 1)], 1.0 / D_MODEL, EPS, ALU.mult, ALU.add)\
                    .then_inc(x_var, 1)
                if att:
                    for q in range(4):
                        dve.wait_ge(s_ps, 4 * b + q + 1)
                        if q == 0:
                            dve.wait_ge(pt_ps, 4 * b + 1)
                        V.scalar_tensor_tensor(E[:, q, :], PS[:, q, :], HEAD_DIM ** -0.5, mask, ALU.mult, ALU.add).then_inc(dve_done, dq.up())
                        dve.wait_ge(dve_done, dq.now())
                        V.reduce_max(mx[:, 2 * q:2 * q + 2], E[:, q, :].rearrange("q (a c) -> q a c", a=2), AX_X).then_inc(dve_done, dq.up())
                    dve.wait_ge(dve_done, dq.now())
                    V.tensor_tensor(mx, mx, sinkb[:, :], ALU.max).then_inc(dve_done, dq.up())
                    dve.wait_ge(dve_done, dq.now())
                    V.tensor_tensor(dsink, sinkb[:, :], mx, ALU.subtract)
                    V.tensor_scalar(nm, mx, -1.0, None, ALU.mult).then_inc(nmax_ok, 1)
                    for q in (1, 3):
                        dve.wait_ge(pt_ps, 4 * b + q + 2)
                        V.tensor_copy(PT[:, q, :], PS[:, q, :]).then_inc(ptd_ok, 1)
                    dve.wait_ge(es_ok, b + 1)
                    dve.wait_ge(exp_ok, 8 * b + 8)
                    V.tensor_tensor(den, rs, es, ALU.add).then_inc(dve_done, dq.up())
                    dve.wait_ge(dve_done, dq.now())
                    V.reciprocal(rinv, den).then_inc(dve_done, dq.up())
                dve.wait_ge(u_ok, t + 1)
                cos = cst[:, ds(t * 64 + K_CS, 32)].rearrange("q (o c) -> q o c", o=1).to_broadcast([P, 20, 32])
                sin = cst[:, ds(t * 64 + (K_CS + 32), 32)].rearrange("q (o c) -> q o c", o=1).to_broadcast([P, 20, 32])
                uv = u_sb.rearrange("q (h c) -> q h c", c=32)
                V.tensor_tensor(t1.rearrange("q (h c) -> q h c", c=32), uv, cos, ALU.mult).then_inc(dve_done, dq.up())
                V.tensor_tensor(t2.rearrange("q (h c) -> q h c", c=32), uv, sin, ALU.mult).then_inc(dve_done, dq.up())
                dve.wait_ge(dve_done, dq.now())
                a4 = t1.rearrange("q (h two c) -> q h two c", two=2, c=32)
                b4 = t2.rearrange("q (h two c) -> q h two c", two=2, c=32)
                r4 = rot[:, p, :].rearrange("q (h two c) -> q h two c", two=2, c=32)
                V.tensor_tensor(r4[:, :, 0, :], a4[:, :, 0, :], b4[:, :, 1, :], ALU.subtract)
                V.tensor_tensor(r4[:, :, 1, :], a4[:, :, 1, :], b4[:, :, 0, :], ALU.add).then_inc(rot_ok, 1)
                if att:
                    dve.wait_ge(o_ps, b + 1)
                    dve.wait_ge(aT_ps, b + 1)
                    dve.wait_ge(ssa_ok, b + 1)
                    V.tensor_tensor(at_st.rearrange("q (h c) -> q h c", c=64), PS[:, 6, :].rearrange("q (h c) -> q h c", c=64),
                                    bc(rinv, 64), ALU.mult).then_inc(attn_ok, 1)
                dve.wait_ge(qkT_ps, 2 * t + 2)
                V.tensor_copy(kT_all[:, ds(t * P + P, P)], PS[:, 5, 2 * P:3 * P]).then_inc(kT_ok, 1)

            step1(0, 0, False, None)
            N1 = 13
            d0 = dq.n
            with dve.Fori(0, 4) as j:
                dq.at(j * 2 * N1 + d0)
                step1(2 * j + 1, 1, True, cst[:, ds((j + 3) // 4 * 512 + K_MASK, 512)])
                assert dq.n == N1, dq.n
                dq.at(j * 2 * N1 + d0 + N1)
                step1(2 * j + 2, 0, True, cst[:, K_MASK + 512:K_MASK + 1024])
                assert dq.n == N1, dq.n
            dq.at(d0 + 8 * N1)

            dve.wait_ge(pt_ps, 4 * NPT + 1)
            dve.wait_ge(x_rstd, NT)
            dg = E.rearrange("q a c -> q (a c)")
            for t in range(NT):
                o = V.tensor_scalar(dg[:, t * P:(t + 1) * P], ident, rsx[:, t:t + 1], None, ALU.mult)
            o.then_inc(diag_ok, 1)
            dve.wait_ge(qz_ok, NT)
            dve.wait_ge(kT_ok, NT)
            V.tensor_copy(Qs, qz[:, 0, :, 0:NDEC].rearrange("q h b -> q b h"))
            V.tensor_copy(kTs[:, :, 0], kT_all[:, P + SEQ:P + SEQ + NDEC]).then_inc(sa_q, 1)
            dve.wait_ge(rbc_ps, 1)
            V.tensor_copy(rbc[:, 0:1024].rearrange("q (a c) -> q a c", a=2), PS[:, 0:2, :])
            V.tensor_copy(rbc[:, 1024:1024 + P], PS[:, 2, 0:P]).then_inc(rbc_ok, 1)
            dve.wait_ge(rbc_ok, 1)
            dve.wait_ge(aT_ps, NPT + 1)
            dve.wait_ge(ssa_ok, NPT + 1)
            dve.wait_ge(qkT_ps, 2 * NT)
            V.memset(xlb[:, 0:CONV - 1], 0.0).then_inc(dve_done, dq.up())
            dve.wait_ge(dve_done, dq.now())
            V.memset(mT_all[:, NFT:KD, TOKENS:], 0.0).then_inc(dve_done, dq.up())
            dve.wait_ge(dve_done, dq.now())

            dve.wait_ge(sa_s, 8)
            V.tensor_scalar(saS[0:8, :].rearrange("q (a c) -> q a c", a=2), PS[0:8, 6:8, :], HEAD_DIM ** -0.5, None,
                                    ALU.mult).then_inc(dve_done, dq.up())
            dve.wait_ge(dve_done, dq.now())
            s3 = saS[0:8, :].rearrange("q (b c) -> q b c", b=NDEC)
            V.reduce_max(sa_mx[0:8, :], s3, AX_X).then_inc(dve_done, dq.up())
            dve.wait_ge(dve_done, dq.now())
            V.tensor_scalar(sa_mx[0:8, :], sa_mx[0:8, :], sinkc[:, :], None, ALU.max).then_inc(sa_s, 1)
            dve.wait_ge(sa_s, 9)

            def bc8(ap):
                return ap.rearrange("q (m o) -> q m o", o=1).to_broadcast([8, NDEC, P])
            V.tensor_tensor(s3, s3, bc8(sa_mx[0:8, :]), ALU.subtract).then_inc(sa_s, 1)
            dve.wait_ge(sa_e, 1)
            V.reduce_sum(sa_sum[0:8, :], s3, AX_X).then_inc(dve_done, dq.up())
            dve.wait_ge(dve_done, dq.now())
            V.tensor_tensor(sa_sum[0:8, :], sa_sum[0:8, :], sa_es[0:8, :], ALU.add).then_inc(dve_done, dq.up())
            dve.wait_ge(dve_done, dq.now())
            V.reciprocal(sa_sum[0:8, :], sa_sum[0:8, :]).then_inc(dve_done, dq.up())
            dve.wait_ge(dve_done, dq.now())
            V.tensor_tensor(s3, s3, bc8(sa_sum[0:8, :]), ALU.mult).then_inc(sa_n, 1)
            dve.wait_ge(par_in, 16 * 8)
            lam = chp[:, :, C_LAM]
            e_, z_, q_ = drv[:, :, 0], drv[:, :, 1], drv[:, :, 2]
            V.tensor_scalar(z_, lam, -1.0, None, ALU.mult).then_inc(dve_done, dq.up())
            dve.wait_ge(dve_done, dq.now())
            V.tensor_tensor(e_, z_, lam, ALU.max).then_inc(expl_ok, 1)
            dve.wait_ge(drv_ok, 1)
            V.tensor_scalar(z_, e_, 2.0, None, ALU.add).then_inc(dve_done, dq.up())
            dve.wait_ge(dve_done, dq.now())
            V.reciprocal(z_, z_).then_inc(dve_done, dq.up())
            dve.wait_ge(dve_done, dq.now())
            V.tensor_tensor(z_, z_, e_, ALU.mult).then_inc(dve_done, dq.up())
            dve.wait_ge(dve_done, dq.now())
            V.tensor_tensor(e_, z_, z_, ALU.mult).then_inc(dve_done, dq.up())
            dve.wait_ge(dve_done, dq.now())
            V.tensor_scalar(q_, e_, 1.0 / 17, 1.0 / 15, ALU.mult, ALU.add).then_inc(dve_done, dq.up())
            dve.wait_ge(dve_done, dq.now())
            for n in (13, 11, 9, 7, 5, 3, 1):
                V.tensor_tensor(q_, q_, e_, ALU.mult).then_inc(dve_done, dq.up())
                dve.wait_ge(dve_done, dq.now())
                V.tensor_scalar(q_, q_, 1.0 / n, None, ALU.add).then_inc(dve_done, dq.up())
                dve.wait_ge(dve_done, dq.now())
            V.tensor_tensor(q_, q_, z_, ALU.mult).then_inc(dve_done, dq.up())
            dve.wait_ge(dve_done, dq.now())
            V.tensor_scalar(z_, lam, -2.0, 0.0, ALU.mult, ALU.max).then_inc(dve_done, dq.up())
            dve.wait_ge(dve_done, dq.now())
            V.scalar_tensor_tensor(q_, q_, 4.0, z_, ALU.mult, ALU.add).then_inc(dve_done, dq.up())
            dve.wait_ge(dve_done, dq.now())
            V.tensor_scalar(drv[:, :, 0], chp[:, :, C_BA], 0.5, None, ALU.mult).then_inc(dve_done, dq.up())
            V.tensor_scalar(drv[:, :, 1], chp[:, :, C_BX], 0.5, None, ALU.mult).then_inc(dve_done, dq.up())
            dve.wait_ge(dve_done, dq.now())
            V.tensor_scalar(drv[:, :, 3], q_, -2.0, None, ALU.mult).then_inc(dve_done, dq.up())
            dve.wait_ge(dve_done, dq.now())
            dve.wait_ge(sa_pt, NDEC)
            V.tensor_copy(saP, PS[:, 6, 0:NDEC * N_HEADS]).then_inc(sa_pte, 1)
            dve.wait_ge(sa_pv, NDEC)
            for lo in range(2):
                half = slice(64 * lo, 64 * lo + 64)
                V.tensor_copy(saT[half], PS[half, 7, 0:64].rearrange("q (b t two) -> q t b two", two=2, b=NDEC)[:, :, :, lo]).then_inc(dve_done, dq.up())
            dve.wait_ge(dve_done, dq.now())
            for lo in range(2):
                half = slice(64 * lo, 64 * lo + 64)
                V.tensor_tensor(mT_all[half, 0:NFT, SEQ:TOKENS], saT[half],
                                gna[half, :].rearrange("q (m o) -> q m o", o=1).to_broadcast([64, NFT, NDEC]), ALU.mult)\
                    .then_inc(sa_m, 1)
            N2 = 15
            base2 = dq.base + dq.n
            with dve.Fori(0, NFT) as f:
                dq.at(f * N2 + base2)
                dve.wait_ge(gate_ok, 6 * f + 1)
                dve.wait_ge(s_ok, f + 1)
                dve.wait_ge(lru_ok, f + 1)
                V.tensor_copy(cp, chp[:, ds(f, 1), :].rearrange("q o c -> q (o c)"))
                V.tensor_copy(dv, drv[:, ds(f, 1), :].rearrange("q o c -> q (o c)")).then_inc(cp_ok, 1)
                dve.wait_ge(cp_ok, f + 1)
                for c in range(3):
                    dve.wait_ge(xl_ps, 3 * f + c + 1)
                    V.tensor_tensor(xlb[:, CONV - 1 + c * CHUNK:CONV - 1 + (c + 1) * CHUNK], PS[:, c, 0:CHUNK],
                                    rbc[:, c * CHUNK:(c + 1) * CHUNK], ALU.mult).then_inc(xl_ok, 1)
                dve.wait_ge(xl_ok, 3 * f + 4)
                for j in range(CONV):
                    wj = cp[:, C_W + j:C_W + j + 1]
                    dst, src = cT[:, 0:SEQ], xlb[:, j:j + SEQ]
                    dds = cT[:, SEQ:TOKENS]
                    srs = cp[:, C_ST + 8 * j:C_ST + 8 * j + 8] if j < CONV - 1 else xlb[:, CONV - 1 + SEQ:CONV - 1 + TOKENS]
                    if j == 0:
                        V.tensor_scalar(dst, src, wj, cp[:, C_B:C_B + 1], ALU.mult, ALU.add).then_inc(dve_done, dq.up())
                        V.tensor_scalar(dds, srs, wj, cp[:, C_B:C_B + 1], ALU.mult, ALU.add).then_inc(dve_done, dq.up())
                        dve.wait_ge(dve_done, dq.now())
                    else:
                        V.scalar_tensor_tensor(dst, src, wj, dst, ALU.mult, ALU.add).then_inc(dve_done, dq.up())
                        V.scalar_tensor_tensor(dds, srs, wj, dds, ALU.mult, ALU.add).then_inc(dve_done, dq.up())
                        dve.wait_ge(dve_done, dq.now())
                V.tensor_copy(smo[:, ds(f, 1), O_XL:O_XL + 3], xlb[:, SEQ:SEQ + 3].rearrange("q (o c) -> q o c", o=1))
                V.tensor_copy(smo[:, ds(f, 1), O_XS:O_XS + 8], xlb[:, CONV - 1 + SEQ:].rearrange("q (o c) -> q o c", o=1))\
                    .then_inc(conv_ok, 1)
                for c in range(3):
                    dve.wait_ge(yg_ps, 3 * f + c + 1)
                    if c == 0:
                        dve.wait_ge(sqb_ok, f + 1)
                    V.tensor_tensor(yb[:, c * CHUNK:(c + 1) * CHUNK], PS[:, 3 + c, 0:CHUNK],
                                    rbc[:, c * CHUNK:(c + 1) * CHUNK], ALU.mult).then_inc(y_ok, 1)
                dve.wait_ge(gate_ok, 6 * f + 7)
                V.scalar_tensor_tensor(tib, tib, 1.0, cT, ALU.add, ALU.mult).then_inc(dve_done, dq.up())
                dve.wait_ge(dve_done, dq.now())
                dve.wait_ge(a_ok, f + 1)
                V.scalar_tensor_tensor(tib, wv, 1.0, tib, ALU.add, ALU.mult).then_inc(dve_done, dq.up())
                dve.wait_ge(dve_done, dq.now())
                dve.wait_ge(sqrt_ok, f + 1)
                V.tensor_tensor(tib, tib, sqh, ALU.mult).then_inc(dve_done, dq.up())
                dve.wait_ge(dve_done, dq.now())
                V.tensor_tensor_scan(sqh[:, 0:SEQ], wv[:, 0:SEQ], tib[:, 0:SEQ], 0.0, ALU.mult, ALU.add).then_inc(dve_done, dq.up())
                V.tensor_tensor(sm8[:, 0, :], wv[:, SEQ:], cp[:, C_H0:C_H0 + 8], ALU.mult).then_inc(dve_done, dq.up())
                dve.wait_ge(dve_done, dq.now())
                V.tensor_tensor(sqh[:, SEQ:], sm8[:, 0, :], tib[:, SEQ:], ALU.add).then_inc(dve_done, dq.up())
                dve.wait_ge(dve_done, dq.now())
                V.tensor_copy(smo[:, ds(f, 1), O_HS:O_HS + 8], sqh[:, SEQ:].rearrange("q (o c) -> q o c", o=1))
                V.tensor_copy(smo[:, ds(f, 1), O_HL:O_HL + 1], sqh[:, SEQ - 1:SEQ].rearrange("q (o c) -> q o c", o=1))
                dve.wait_ge(th_ok, f + 1)
                V.scalar_tensor_tensor(inn, inn, 1.0, yb, ALU.add, ALU.mult).then_inc(dve_done, dq.up())
                dve.wait_ge(dve_done, dq.now())
                V.scalar_tensor_tensor(yb, inn, 0.5, sqh, ALU.mult, ALU.mult).then_inc(out_ok, 1)
                dve.wait_ge(out_ok, f + 1)
                V.tensor_scalar(mT_all[:, ds(f + NFT, 1), 0:TOKENS].rearrange("q o c -> q (o c)"), yb,
                                cp[:, C_GN:C_GN + 1], None, ALU.mult).then_inc(lru_ok, 1)
                assert dq.n == N2, dq.n
            dq.at(base2 + NFT * N2)

            dve.wait_ge(ss_ps, 1)
            V.tensor_copy(ssl[:, 0:NPT], PS[:, 4, 0:NPT]).then_inc(dve_done, dq.up())
            V.tensor_copy(ssl[0:8, NPT:NT], PS[0:8, 4, NPT:NT]).then_inc(dve_done, dq.up())
            V.tensor_copy(ssa[0:8, NPT:NT], PS[0:8, 4, 16:17]).then_inc(dve_done, dq.up())
            dve.wait_ge(dve_done, dq.now())
            V.tensor_scalar(val, ssa, 1.0 / ATTN, EPS, ALU.mult, ALU.add)
            V.tensor_scalar(val2[:, 0, :], ssl, 1.0 / LRU, EPS, ALU.mult, ALU.add).then_inc(varal_ok, 1)
            V.memset(cnt, 0.0).then_inc(dve_done, dq.up())
            dve.wait_ge(dve_done, dq.now())
            V.memset(lg, -3e38).then_inc(dve_done, dq.up())
            dve.wait_ge(dve_done, dq.now())
            dve.wait_ge(ral_ok, 2)

            def x2_half(t, p, n, rounds):
                if n == 0:
                    dve.wait_ge(x_in2[p], 16 * rounds)
                cols = slice(512 * n, 512 * n + 512)
                dve.wait_ge(op_ps, 2 * t + n + 1)
                if not isinstance(t, int) or t > 0 or n > 0:
                    dve.wait_ge(x2_ok, 2 * t + n)
                V.scalar_tensor_tensor(x2t, PS[:, 2 * n, :], ral[:, ds(t, 1)], xin[:, p, cols], ALU.mult, ALU.add).then_inc(dve_done, dq.up())
                dve.wait_ge(dve_done, dq.now())
                V.scalar_tensor_tensor(x2_all[:, ds(t, 1), cols].rearrange("q o c -> q (o c)"), PS[:, 2 * n + 1, :],
                                       val2[:, 1, ds(t, 1)], x2t, ALU.mult, ALU.add).then_inc(x2_ok, 1)

            def norm2(t, p, rounds):
                dve.wait_ge(ss2_ok, t + 2)
                V.tensor_scalar(var2[:, ds(t, 1)], ss2[:, ds(t, 1)], 1.0 / D_MODEL, EPS, ALU.mult, ALU.add)\
                    .then_inc(var2_ok, 1)
                dve.wait_ge(rs2_ok, t + 1)
                if not (isinstance(rounds, int) and rounds == 0):
                    dve.wait_ge(xt_out[p], 16 * rounds)
                V.scalar_tensor_tensor(xn[:, p, :], x2_all[:, ds(t, 1), :].rearrange("q o c -> q (o c)"), rs2[:, ds(t, 1)],
                                       g2b, ALU.mult, ALU.mult).then_inc(xn_ok, 1)

            def route(t):
                dve.wait_ge(xT2_ps, 2 * t + 2)
                V.tensor_copy(xT2[:, 4:8, :], PS[:, 5, :].rearrange("q (a c) -> q a c", a=4)).then_inc(xT2d_ok, 1)
                dve.wait_ge(r_ps, t + 1)
                if not isinstance(t, int) or t > 0:
                    dve.wait_ge(idx_ok, t)
                V.tensor_tensor(lg[:, 0:4], PS[:, 6, 0:4], brb[:, 0:4], ALU.add).then_inc(dve_done, dq.up())
                V.tensor_tensor(le, PS[:, 6, 4:NR], brb[:, 4:NR], ALU.add).then_inc(dve_done, dq.up())
                dve.wait_ge(dve_done, dq.now())
                alone(dve)
                V.max(top, lg).then_inc(dve_done, dq.up())
                dve.wait_ge(dve_done, dq.now())
                alone(dve)
                V.max_index(idxg[:, :], top, lg).then_inc(dve_done, dq.up())
                V.tensor_scalar(sc[:, 0:1], top[:, 0:1], -1.0, None, ALU.mult).then_inc(lgx_ok, 1)
                dve.wait_ge(dve_done, dq.now())
                V.tensor_copy(sc[:, 4:5], idxg[:, 0:1]).then_inc(dve_done, dq.up())
                dve.wait_ge(dve_done, dq.now())
                V.tensor_scalar(ohg, cst[:, K_IE:K_IE + 4], sc[:, 4:5], None, ALU.is_equal).then_inc(dve_done, dq.up())
                dve.wait_ge(dve_done, dq.now())
                V.tensor_tensor(lem, le.rearrange("q (g e) -> q e g", g=N_GROUPS),
                                        ohg.rearrange("q (o g) -> q o g", o=1).to_broadcast([P, N_PER_GROUP, N_GROUPS]), ALU.mult).then_inc(dve_done, dq.up())
                dve.wait_ge(dve_done, dq.now())
                V.reduce_sum(les, lem, AX_X).then_inc(dve_done, dq.up())
                dve.wait_ge(dve_done, dq.now())
                alone(dve)
                V.max(toe, les).then_inc(dve_done, dq.up())
                dve.wait_ge(dve_done, dq.now())
                alone(dve)
                V.max_index(idxp[:, :], toe, les).then_inc(dve_done, dq.up())
                V.tensor_scalar(sc[:, 2:3], toe[:, 0:1], -1.0, None, ALU.mult).then_inc(top_ok, 1)
                dve.wait_ge(dve_done, dq.now())
                V.tensor_copy(rr[:, 0, :], idxp[:, 0:2]).then_inc(dve_done, dq.up())
                dve.wait_ge(dve_done, dq.now())
                V.tensor_scalar(sc[:, 4:5], sc[:, 4:5], float(N_PER_GROUP), None, ALU.mult).then_inc(dve_done, dq.up())
                dve.wait_ge(dve_done, dq.now())
                V.tensor_scalar(rr[:, 0, :], rr[:, 0, :], sc[:, 4:5], None, ALU.add).then_inc(dve_done, dq.up())
                dve.wait_ge(dve_done, dq.now())
                for k in range(TOPK):
                    V.tensor_scalar(oh[:, k, :], cst[:, K_IE:K_IE + NE], rr[:, 0, k:k + 1], None, ALU.is_equal).then_inc(dve_done, dq.up())
                dve.wait_ge(dve_done, dq.now())
                V.tensor_tensor(M, oh[:, 0, :], oh[:, 1, :], ALU.add).then_inc(dve_done, dq.up())
                dve.wait_ge(dve_done, dq.now())
                V.tensor_scalar(M, M, cst[:, ds(t + K_VALID, 1)], None, ALU.mult).then_inc(M_ok, 1)
                dve.wait_ge(ege_ok, t + 1)
                dve.wait_ge(eexp_ok, t + 1)
                V.tensor_scalar(sc[:, 6:7], sc[:, 3:4], 1.0, None, ALU.add).then_inc(dve_done, dq.up())
                dve.wait_ge(dve_done, dq.now())
                V.tensor_tensor(sc[:, 6:7], sc[:, 6:7], sc[:, 1:2], ALU.mult).then_inc(dve_done, dq.up())
                dve.wait_ge(dve_done, dq.now())
                V.reciprocal(sc[:, 7:8], sc[:, 6:7]).then_inc(dve_done, dq.up())
                dve.wait_ge(dve_done, dq.now())
                V.tensor_copy(comb[:, ds(t, 1), 0:1], sc[:, 7:8].rearrange("q (o c) -> q o c", o=1)).then_inc(dve_done, dq.up())
                V.tensor_tensor(comb[:, ds(t, 1), 1:2], sc[:, 7:8].rearrange("q (o c) -> q o c", o=1),
                                sc[:, 3:4].rearrange("q (o c) -> q o c", o=1), ALU.mult).then_inc(dve_done, dq.up())
                dve.wait_ge(rk_ps, t + 1)
                V.tensor_tensor(rk, PS[:, 7, 0:NE], cnt, ALU.add).then_inc(dve_done, dq.up())
                V.tensor_tensor(cnt, PS[:, 7, NE:2 * NE], cnt, ALU.add).then_inc(dve_done, dq.up())
                dve.wait_ge(dve_done, dq.now())
                V.tensor_tensor(jnk32, oh, rk.rearrange("q (o c) -> q o c", o=1).to_broadcast([P, TOPK, NE]), ALU.mult).then_inc(dve_done, dq.up())
                dve.wait_ge(dve_done, dq.now())
                V.reduce_sum(rr[:, 1, :], jnk32, AX_X).then_inc(dve_done, dq.up())
                dve.wait_ge(dve_done, dq.now())
                V.tensor_tensor(thrq, cst[:, K_THR:K_THR + 8].rearrange("q (o c) -> q o c", o=1)
                                        .to_broadcast([P, TOPK, 8]), bc(rr[:, 1, :], 8), ALU.is_le).then_inc(dve_done, dq.up())
                dve.wait_ge(dve_done, dq.now())
                V.reduce_sum(rr[:, 2, :], thrq, AX_X).then_inc(dve_done, dq.up())
                dve.wait_ge(dve_done, dq.now())
                row = NE * MAXC
                V.tensor_scalar(rr[:, 3, :], rr[:, 0, :], float(MAXC), None, ALU.mult).then_inc(dve_done, dq.up())
                dve.wait_ge(dve_done, dq.now())
                V.scalar_tensor_tensor(rr[:, 3, :], rr[:, 2, :], float(1 - CAP * row), rr[:, 3, :], ALU.mult, ALU.add).then_inc(dve_done, dq.up())
                dve.wait_ge(dve_done, dq.now())

            def place(t, p, rounds):
                if not (isinstance(rounds, int) and rounds == 0):
                    dve.wait_ge(scat[p], 32 * rounds)
                V.scalar_tensor_tensor(idxs[:, p, :], rr[:, 1, :], float(NE * MAXC), rr[:, 3, :], ALU.mult, ALU.add)\
                    .then_inc(idx_ok, 1)

            N3 = 31
            x2_half(0, 0, 0, 1)
            dve.wait_ge(pre_in, 16)
            base3 = dq.base + dq.n
            dq.at(base3)

            def step3(t, p, rounds):
                x2_half(t, p, 1, None)
                norm2(t, p, rounds[0])
                if rounds[1] is not None:
                    x2_half(t + 1, 1 - p, 0, rounds[1])
                route(t)
                place(t, p, rounds[0])

            step3(0, 0, (0, 1))
            assert dq.n == N3, dq.n
            dq.at(base3 + N3)
            step3(1, 1, (0, 2))
            with dve.Fori(0, 3) as j:
                dq.at(j * 2 * N3 + base3 + 2 * N3)
                step3(2 * j + 2, 0, (j + 1, j + 2))
                dq.at(j * 2 * N3 + base3 + 3 * N3)
                step3(2 * j + 3, 1, (j + 1, j + 3))
            dq.at(base3 + 8 * N3)
            step3(8, 0, (4, None))
            V.tensor_tensor(bigc, bc(cnt, 8), cst[:, K_THR:K_THR + 8].rearrange("q (o c) -> q o c", o=1)
                                    .to_broadcast([P, NE, 8]), ALU.is_gt).then_inc(dve_done, dq.up())
            dve.wait_ge(dve_done, dq.now())
            V.reduce_sum(xe, bigc, AX_X).then_inc(dve_done, dq.up())
            dve.wait_ge(dve_done, dq.now())
            V.tensor_tensor_scan(incl, ones[:, 0:NE], xe, 0.0, ALU.mult, ALU.add).then_inc(dve_done, dq.up())
            dve.wait_ge(dve_done, dq.now())
            V.tensor_tensor(lev, incl.rearrange("q (o c) -> q o c", o=1).to_broadcast([P, MAXV, NE]),
                                    bc(cst[:, K_IV:K_IV + MAXV], NE), ALU.is_le).then_inc(dve_done, dq.up())
            dve.wait_ge(dve_done, dq.now())
            V.tensor_tensor(lex, lev, xe.rearrange("q (o c) -> q o c", o=1).to_broadcast([P, MAXV, NE]), ALU.mult).then_inc(dve_done, dq.up())
            V.reduce_sum(ev[:, 0, :], lev, AX_X).then_inc(dve_done, dq.up())
            dve.wait_ge(dve_done, dq.now())
            V.reduce_sum(ev[:, 1, :], lex, AX_X).then_inc(dve_done, dq.up())
            dve.wait_ge(dve_done, dq.now())
            V.tensor_tensor(ev[:, 1, :], cst[:, K_IV:K_IV + MAXV], ev[:, 1, :], ALU.subtract).then_inc(dve_done, dq.up())
            dve.wait_ge(dve_done, dq.now())
            V.scalar_tensor_tensor(ev[:, 1, :], ev[:, 0, :], float(MAXC), ev[:, 1, :], ALU.mult, ALU.add).then_inc(dve_done, dq.up())
            dve.wait_ge(dve_done, dq.now())
            V.tensor_scalar(ev[:, 1, :], ev[:, 1, :], 1.0, None, ALU.add).then_inc(dve_done, dq.up())
            dve.wait_ge(dve_done, dq.now())
            V.tensor_copy(vtab[:, 0:2 * MAXV], ev[0:1].rearrange("q a c -> q (a c)"))
            V.tensor_copy(vtab[:, 2 * MAXV:2 * MAXV + 1], incl[0:1, NE - 1:NE]).then_inc(vtab_ok, 1)
            dve.wait_ge(vtab_ok, 1)
            for p in range(2):
                dve.wait_ge(xt_out[p], 16 * (5 - p))
            dve.wait_ge(op_ps, 2 * NT)
            V.memset(thrq, 0.0).then_inc(cnt_ok, 1)

            def unit_h(u):
                n, p2, p3, r2, r3 = u
                dve.wait_ge(th2_ok, n + 1)
                V.scalar_tensor_tensor(hh[:, p2, :], hh[:, p2, :], 1.0, PS[:, 2 + p2, 0:D_EXPERT], ALU.add, ALU.mult)\
                    .then_inc(hg_ok, 1)
                dve.wait_ge(hg_ok, n + 1)
                V.scalar_tensor_tensor(hh[:, p2, :], hh[:, p2, :], 0.5, PS[:, 2 + p2, D_EXPERT:2 * D_EXPERT], ALU.mult,
                                       ALU.mult).then_inc(h_ok, 1)

            def unit_x(u):
                n, p2, p3, r2, r3 = u
                dve.wait_ge(xgT_ps, 2 * n + 2)
                V.tensor_copy(xgT[:, p2, 4:8, :], PS[:, 1, :].rearrange("q (a c) -> q a c", a=4)).then_inc(xgd_ok, 1)

            def unit_y(u):
                n, p2, p3, r2, r3 = u
                if not isinstance(n, int) or n >= 2:
                    dve.wait_ge(yo_out[p2], 16 * r2)
                dve.wait_ge(y_ps, 2 * n + 2)
                V.tensor_copy(yo[:, p2, 512:1024], PS[:, 6, :]).then_inc(yod_ok, 1)

            unit_x(unit(0, 0))
            unit_h(unit(0, 0))
            unit_x(unit(0, 1))

            def step4(j, i, more):
                unit_h(unit(j, i + 1))
                if more:
                    unit_x(unit(j, i + 2))
                unit_y(unit(j, i))
            for i in range(6):
                step4(0, i, True)
            with dve.Fori(1, 5) as j:
                for i in range(6):
                    step4(j, i, True)
            step4(5, 0, False)
            unit_y(unit(5, 1))
            nv = dve.value_load(vtab[0:1, 2 * MAXV:2 * MAXV + 1], min_val=0, max_val=MAXV)
            with dve.If(nv > 0):
                with dve.Fori(0, nv) as v:
                    unit_x(further(v))
                    unit_h(further(v))
                    unit_y(further(v))
                dve.wait_ge(vtab_ok, 1)

            def add_y(t):
                dve.wait_ge(yp_in[t % 4], 16 * (t // 4 + 1))
                x2 = x2_all[:, t, :]
                V.scalar_tensor_tensor(x2, yp[:, t % 4, 0:D_MODEL], comb[:, t, 0:1], x2, ALU.mult, ALU.add).then_inc(x3a, 1)
                dve.wait_ge(x3a, t + 1)
                V.scalar_tensor_tensor(x2, yp[:, t % 4, D_MODEL:], comb[:, t, 1:2], x2, ALU.mult, ALU.add).then_inc(x3_ok, 1)

            def finish(t):
                dve.wait_ge(rs3_ok, t + 1)
                if t >= 2:
                    dve.wait_ge(o_out[t % 2], 16 * (t // 2))
                V.scalar_tensor_tensor(ob[:, t % 2, :], x2_all[:, t, :], rs3[:, t:t + 1], gfb, ALU.mult, ALU.mult)\
                    .then_inc(ob_ok, 1)

            def mean(t):
                dve.wait_ge(ss3_ok, t + 2)
                V.tensor_scalar(ss3[:, t:t + 1], ss3[:, t:t + 1], 1.0 / D_MODEL, EPS, ALU.mult, ALU.add).then_inc(var3_ok, 1)

            add_y(0)
            mean(0)
            dve.wait_ge(gf_in, 16)
            for t in range(NT):
                if t + 1 < NT:
                    add_y(t + 1)
                finish(t)
                if t + 1 < NT:
                    mean(t + 1)

        @block.tensor
        def _(pe):
            MM, TR = nc.tensor.matmul, nc.tensor.transpose
            for first_pass in (pt_ps, aT_ps):
                pe.sem_inc(first_pass, 1)

            def step1(t, p, rounds, att):
                b = t - 1
                pe.wait_ge(x_in[p], 16 * rounds)
                for k in range(KD):
                    o = TR(PS[:, 2 + k // 4, (k % 4) * P:(k % 4 + 1) * P], xin[:, p, k * P:(k + 1) * P], ident)
                    if k % 4 == 3:
                        o.then_inc(xT_ps, 1)
                if att:
                    pe.wait_ge(qz_ok, t)
                    pe.wait_ge(kT_ok, t)
                    for q in range(4):
                        if q >= 2:
                            pe.wait_ge(xs_ok, 2 * t + q - 1)
                        for h in range(2):
                            o = MM(PS[:, q, 256 * h:256 * h + 256], qz[:, 1 - p, 2 * q + h, :], kT_all[:, ds(b * P, 2 * P)],
                                   start=True, stop=True)
                        o.then_inc(s_ps, 1)
                pe.wait_ge(xs_ok, 2 * t + 2)
                for k in range(KD):
                    if k % (KD // 2) == 0 and not att:
                        pe.wait_ge(wqkv_in[k // (KD // 2)], 16)
                    MM(PS[:, 4, :], xs[:, p, k, :], wqkv[:, k, 0:ATTN], start=(k == 0), stop=(k == KD - 1))
                    o = MM(PS[:, 5, 0:2 * KV], xs[:, p, k, :], wqkv[:, k, ATTN:QKV], start=(k == 0), stop=(k == KD - 1))
                o.then_inc(qkv_ps, 1)
                if att:
                    for q in range(4):
                        pe.wait_ge(exp_ok, 8 * b + 2 * q + 2)
                        for c in range(4):
                            o = TR(PS[:, q, c * P:(c + 1) * P], E[:, q, c * P:(c + 1) * P], ident)
                        o.then_inc(pt_ps, 1)
                    pe.wait_ge(aT_ok, b + 1)
                    pe.wait_ge(v_ok, t)
                    for q in range(4):
                        pe.wait_ge(ptd_ok if q % 2 else pta_ok, 2 * b + q // 2 + 1)
                        for h in range(2):
                            for kk in range(2):
                                o = MM(PS[:, 6, q * P + 64 * h:q * P + 64 * h + 64], PT[:, q, (2 * h + kk) * P:(2 * h + kk + 1) * P],
                                       v_all[:, ds(b + kk, 1), 64 * h:64 * h + 64].rearrange("q o c -> q (o c)"),
                                       start=(kk == 0), stop=(kk == 1))
                    o.then_inc(o_ps, 1)
                pe.wait_ge(rot_ok, t + 1)
                pe.wait_ge(v_ok, t + 1)
                for k in range(4):
                    o = TR(PS[:, 7, k * P:(k + 1) * P], rot[:, p, k * P:(k + 1) * P], ident)
                o.then_inc(qkT_ps, 1)
                TR(PS[:, 5, 2 * P:3 * P], rot[:, p, ATTN:], ident).then_inc(qkT_ps, 1)
                if att:
                    pe.wait_ge(attn_ok, b + 1)
                    for k in range(4):
                        o = TR(PS[:, 6, k * P:(k + 1) * P], at_st[:, k * P:(k + 1) * P], ident)
                    o.then_inc(aT_ps, 1)

            pe.wait_ge(id_in, 16)
            pe.wait_ge(mem0, 7)
            step1(0, 0, 1, False)
            with pe.Fori(0, 4) as j:
                step1(2 * j + 1, 1, j + 1, True)
                step1(2 * j + 2, 0, j + 2, True)

            pe.wait_ge(diag_ok, 1)
            dg = E.rearrange("q a c -> q (a c)")
            MM(PS[:, 0, :], ones[:, :], dg[:, 0:512], start=True, stop=True)
            MM(PS[:, 1, :], ones[:, :], dg[:, 512:1024], start=True, stop=True)
            MM(PS[:, 2, 0:P], ones[:, :], dg[:, 1024:1024 + P], start=True, stop=True).then_inc(rbc_ps, 1)
            pe.wait_ge(rbc_ok, 1)
            pe.wait_ge(aT_ok, NPT + 1)
            pe.wait_ge(xTall_ok, NT + 1)

            pe.wait_ge(sa_q, 1)
            for b in range(NDEC):
                MM(PS[0:8, 6 + b // 4, (b % 4) * P:(b % 4 + 1) * P], Qs[:, b, :], kTs[:, b, :], start=True, stop=True)\
                    .then_inc(sa_s, 1)

            def decode_values():
                pe.wait_ge(sa_n, 1)
                for b in range(NDEC):
                    MM(PS[:, 6, 8 * b:8 * b + 8], saS[0:8, b * P:(b + 1) * P], ident[0:8, 0:8], start=True, stop=True)\
                        .then_inc(sa_pt, 1)
                pe.wait_ge(vnew_in, 16)
                pe.wait_ge(sa_pte, 1)
                for b in range(NDEC):
                    MM(PS[:, 7, 8 * b:8 * b + 8], Vs[:, b, :], saP[:, 8 * b:8 * b + 8], start=True, stop=True)\
                        .then_inc(sa_pv, 1)

            for f in range(NFT):
                p = f % 2
                pe.wait_ge(wxy_in[p], 32 * (f // 2) + 32)
                pe.wait_ge(xl_ok, 3 * f + 1)
                for k in range(KD):
                    for c in range(3):
                        o = MM(PS[:, c, 0:CHUNK], wxy[p][:, k, 0:P], xT_all[:, k, c * CHUNK:(c + 1) * CHUNK],
                               start=(k == 0), stop=(k == KD - 1))
                        if k == KD - 1:
                            o.then_inc(xl_ps, 1)
                if f == 0:
                    decode_values()
                pe.wait_ge(y_ok, 3 * f + 1)
                for k in range(KD):
                    for c in range(3):
                        o = MM(PS[:, 3 + c, 0:CHUNK], wxy[p][:, k, P:2 * P], xT_all[:, k, c * CHUNK:(c + 1) * CHUNK],
                               start=(k == 0), stop=(k == KD - 1))
                        if k == KD - 1:
                            o.then_inc(yg_ps, 1)
                pe.wait_ge(conv_ok, f + 1)
                for c in range(3):
                    for g in range(2):
                        if c == 0 and g == 0:
                            pe.wait_ge(gate_ok, 6 * f + 1)
                        elif c > 0:
                            pe.wait_ge(gate_ok, 6 * f + 2 * (c - 1) + g + 2)
                        MM(PS[:, 6 + g, 0:CHUNK], wgate[:, p, g * P:(g + 1) * P], cT[:, c * CHUNK:(c + 1) * CHUNK],
                           start=True, stop=True).then_inc(gt_ps, 1)

            def op_quarter(t, p, n, g):
                if n == 0 and g == 0 and not (isinstance(t, int) and t == 0):
                    pe.wait_ge(mts_ok, t + 1)
                if not isinstance(t, int) or t > 0:
                    pe.wait_ge(x2_ok, 2 * t - 1 + n)
                for k in range(4):
                    o = MM(PS[:, 2 * n + g, :], mTs[:, p, 4 * g + k, :], wout[:, 4 * g + k, 512 * n:512 * n + 512],
                           start=(k == 0), stop=(k == 3))
                if g == 1:
                    o.then_inc(op_ps, 1)

            pe.wait_ge(xl_ok, 3 * NFT + 1)
            pe.wait_ge(wout_in[0], 16)
            pe.wait_ge(mta_ok, 1)
            for n in range(2):
                op_quarter(0, 0, n, 0)
            pe.wait_ge(y_ok, 3 * NFT + 1)
            pe.wait_ge(sqacc_ok, 1)
            for t in range(NT):
                rows = P if t < NPT else NDEC
                MM(PS[0:rows, 4, t:t + 1], sqacc[:, t * P:t * P + rows], ones[:, 0:1], start=True, stop=True)
            pe.wait_ge(sa_sq, 1)
            for k in range(NFT):
                o = MM(PS[0:NDEC, 4, 16:17], saP[:, 8 * k:8 * k + 8], ones[:, 0:1], start=(k == 0), stop=(k == NFT - 1))
            o.then_inc(ss_ps, 1)

            def xT2_(t, p):
                pe.wait_ge(xn_ok, t + 1)
                for k in range(KD):
                    o = TR(PS[:, 4 + k // 4, (k % 4) * P:(k % 4 + 1) * P], xn[:, p, k * P:(k + 1) * P], ident)
                    if k % 4 == 3:
                        o.then_inc(xT2_ps, 1)

            def router(t):
                pe.wait_ge(xT2a_ok, t + 1)
                pe.wait_ge(xT2d_ok, t + 1)
                for k in range(KD):
                    o = MM(PS[:, 6, 0:NR], xT2[:, k, :], wr[:, k, :], start=(k == 0), stop=(k == KD - 1))
                o.then_inc(r_ps, 1)

            def ranks(t):
                pe.wait_ge(M_ok, t + 1)
                MM(PS[:, 7, 0:NE], upper, M, start=True, stop=True)
                MM(PS[:, 7, NE:2 * NE], ones[:, :], M, start=True, stop=True).then_inc(rk_ps, 1)

            def step3(t, p):
                op_quarter(t + 1, 1 - p, 0, 0)
                op_quarter(t + 1, 1 - p, 0, 1)
                xT2_(t, p)
                router(t)
                op_quarter(t + 1, 1 - p, 1, 0)
                ranks(t)
                op_quarter(t + 1, 1 - p, 1, 1)
            pe.wait_ge(mts_ok, 1)
            pe.wait_ge(wout_in[1], 16)
            for n in range(2):
                op_quarter(0, 0, n, 1)
            pe.wait_ge(varal_ok, 1)
            with pe.Fori(0, 4) as j:
                step3(2 * j, 0)
                step3(2 * j + 1, 1)
            xT2_(8, 0)
            router(8)
            ranks(8)

            pe.wait_ge(cnt_ok, 1)

            def unit_x(u):
                n, p2, p3, r2, r3 = u
                pe.wait_ge(xg_in[p3], 16 * r3 + 16)
                if not isinstance(n, int) or n > 0:
                    pe.wait_ge(xga_ok, n)
                    pe.wait_ge(xgd_ok, n)
                for k in range(KD):
                    o = TR(PS[:, k // 4, (k % 4) * P:(k % 4 + 1) * P], xg[:, p3, k * P:(k + 1) * P], ident)
                    if k % 4 == 3:
                        o.then_inc(xgT_ps, 1)

            def unit_gu(u):
                n, p2, p3, r2, r3 = u
                pe.wait_ge(wexp_in[p3], 16 * r3 + 16)
                for k in range(KD):
                    if k == 0:
                        pe.wait_ge(xga_ok, n + 1)
                    if k == 4:
                        pe.wait_ge(xgd_ok, n + 1)
                    o = MM(PS[:, 2 + p2, :], xgT[:, p2, k, :], wexp[p3][:, k * 512:(k + 1) * 512],
                           start=(k == 0), stop=(k == KD - 1))
                o.then_inc(gu_ps, 1)

            def unit_hT(u):
                n, p2, p3, r2, r3 = u
                pe.wait_ge(h_ok, n + 1)
                for k in range(KF):
                    o = TR(PS[:, 4, k * P:(k + 1) * P], hh[:, p2, k * P:(k + 1) * P], ident)
                o.then_inc(hT_ps, 1)

            def unit_y(u):
                n, p2, p3, r2, r3 = u
                pe.wait_ge(hTa_ok, n + 1)
                for half in range(2):
                    pe.wait_ge(yod_ok if half else yoa_ok, n + 1)
                    for k in range(KF):
                        at = KD * 512 + k * D_MODEL + half * 512
                        o = MM(PS[:, 5 + half, :], hT[:, p2, k, :], wexp[p3][:, at:at + 512],
                               start=(k == 0), stop=(k == KF - 1))
                    o.then_inc(y_ps, 1)

            unit_x(unit(0, 0))
            unit_gu(unit(0, 0))
            unit_x(unit(0, 1))
            unit_hT(unit(0, 0))

            def step4(j, i, more):
                unit_gu(unit(j, i + 1))
                if more:
                    unit_x(unit(j, i + 2))
                unit_y(unit(j, i))
                unit_hT(unit(j, i + 1))
            with pe.Fori(0, 5) as j:
                for i in range(6):
                    step4(j, i, True)
            step4(5, 0, False)
            unit_y(unit(5, 1))
            pe.wait_ge(vtab_ok, 1)
            nv = pe.value_load(vtab[0:1, 2 * MAXV:2 * MAXV + 1], min_val=0, max_val=MAXV)
            with pe.If(nv > 0):
                with pe.Fori(0, nv) as v:
                    unit_x(further(v))
                    unit_gu(further(v))
                    unit_hT(further(v))
                    unit_y(further(v))
                pe.wait_ge(vtab_ok, 1)


def constants():
    c = np.zeros((P, K_N), np.float32)
    c[:, K_ID:K_ID + P] = np.eye(P)
    c[:, K_UP:K_UP + P] = np.triu(np.ones((P, P)), 1)
    r, k = np.arange(P)[:, None], np.arange(2 * P)[None, :]
    seen = (k > r) & (k <= r + P)
    for kind, ok in enumerate((seen & (k >= P), seen)):
        m = np.where(ok, 0.0, MASKED)
        c[:, K_MASK + 512 * kind:K_MASK + 512 * (kind + 1)] = np.concatenate([m, m], 1)
    inv = 10000.0 ** (-2.0 * np.arange(32) / HEAD_DIM)
    for t in range(NT):
        pos = t * P + np.arange(P) if t < NPT else np.full(P, PAST_LEN)
        ang = pos.astype(np.float32)[:, None] * inv.astype(np.float32)[None, :]
        c[:, K_CS + 64 * t:K_CS + 64 * t + 32] = np.cos(ang)
        c[:, K_CS + 64 * t + 32:K_CS + 64 * t + 64] = np.sin(ang)
    c[:, K_THR:K_THR + 8] = CAP * np.arange(1, 9)
    c[:, K_IE:K_IE + NE] = np.arange(NE)
    c[:, K_IV:K_IV + MAXV] = np.arange(MAXV)
    c[:, K_VALID:K_VALID + NT] = 1.0
    c[NDEC:, K_VALID + NPT] = 0.0
    tok = (np.arange(NT)[None, :] * P + np.arange(P)[:, None]).astype(np.int32)
    pay = np.stack([tok, 2 * tok, tok, 2 * tok + 1], -1).astype(np.int32)
    return c, pay


def layout(inputs):
    n = {k: np.asarray(v) for k, v in inputs.items()}
    pair = [0, 4, 1, 5, 2, 6, 3, 7]
    cst, pay = constants()
    w_in = n["w_in"][0]
    q = w_in[:, :ATTN].reshape(D_MODEL, N_HEADS, HEAD_DIM)[:, pair].reshape(D_MODEL, ATTN)
    wqkv = np.concatenate([q, w_in[:, ATTN:QKV]], 1)

    def tiles(m):
        return np.ascontiguousarray(m.reshape(-1, P, m.shape[1]).transpose(1, 0, 2))

    xl, yg = w_in[:, QKV:QKV + LRU], w_in[:, QKV + LRU:]
    wxy = np.stack([tiles(np.concatenate([xl[:, f * P:(f + 1) * P], yg[:, f * P:(f + 1) * P]], 1)) for f in range(NFT)])
    wg = np.zeros((NFT, P, 2 * P), np.float32)
    for g, name in enumerate(("w_rg_a", "w_rg_x")):
        for h in range(N_HEADS):
            f, o = h // 2, 64 * (h % 2)
            wg[f, o:o + 64, g * P + o:g * P + o + 64] = n[name][0, h]

    def chan(v):
        return v.reshape(NFT, P, -1).transpose(1, 0, 2)
    chp = np.concatenate([
        chan(n["w_conv"][0].T), chan(n["b_conv"][0]), chan(n["b_rg_a"][0]), chan(n["b_rg_x"][0]), chan(n["lru_lambda"][0]),
        chan(n["gn_lru"][0]), chan(n["state_conv"][0].transpose(2, 1, 0).reshape(LRU, 24)), chan(n["state_lru_h"][0].T)], 2)
    gna = n["gn_attn"][0].reshape(N_HEADS, HEAD_DIM)[pair].reshape(NFT, P).T
    wo = n["w_out"][0]
    woa = wo[:ATTN].reshape(N_HEADS, HEAD_DIM, D_MODEL)[pair].reshape(ATTN, D_MODEL)
    wgu = np.concatenate([n["w_exp_gate"][0], n["w_exp_up"][0]], -1).reshape(NE, KD, P, 2 * D_EXPERT)
    wd = n["w_exp_down"][0].reshape(NE, KF, P, D_MODEL)
    wexp = np.concatenate([wgu.transpose(0, 2, 1, 3).reshape(NE, P, -1), wd.transpose(0, 2, 1, 3).reshape(NE, P, -1)], 2)
    ck, cv = n["cache_k_win"][0], n["cache_v_win"][0]
    out = {
        "x": np.concatenate([n["x_prompt"][0], n["x_sample"][:, 0]], 0),
        "cst": cst, "payload": pay, "g1": n["ln1_g"][0].reshape(KD, P).T, "gna": gna,
        "sinkc": n["attn_sinks"][0][pair][:, None], "sinks": n["attn_sinks"][0][pair], "chp": chp,
        "wr": tiles(np.concatenate([n["w_router_grp"][0], n["w_router_exp"][0]], 1)),
        "kTs": ck.reshape(NDEC, WINDOW, KV).transpose(2, 0, 1), "Vs": cv.reshape(NDEC, WINDOW, KV).transpose(1, 0, 2),
        "b_router": np.concatenate([n["b_router_grp"][0], n["b_router_exp"][0]]),
        "g2": n["ln2_g"][0], "gf": n["final_g"], "wqkv": tiles(wqkv), "wxy": wxy, "wgate": wg,
        "wout": tiles(np.concatenate([woa, wo[ATTN:]], 0)), "wexp": wexp,
        "conv_old": n["state_conv"][0], "cache_k": ck.reshape(NDEC, WINDOW, KV), "cache_v": cv.reshape(NDEC, WINDOW, KV),
    }
    return {k: np.ascontiguousarray(v) for k, v in out.items()}


OUTS = {"y": (TOKENS, D_MODEL), "p_k": (WINDOW, KV), "p_v": (WINDOW, KV), "s_k": (NDEC, WINDOW, KV),
        "s_v": (NDEC, WINDOW, KV), "s_c": (NDEC, CONV - 2, LRU), "rec": (P, NFT, O_N)}


def kernel(**inputs):
    import concourse.bacc as bacc
    from concourse.bass_utils import run_bass_kernel_spmd as run

    arrays = layout(inputs)
    nc = bacc.Bacc("TRN2", target_bir_lowering=False, num_devices=1)
    aps = {k: nc.dram_tensor("in_" + k, v.shape, mybir.dt.from_np(v.dtype), kind="ExternalInput").ap() for k, v in arrays.items()}
    aps.update({k: nc.dram_tensor("out_" + k, s, F32, kind="ExternalOutput").ap() for k, s in OUTS.items()})
    build(nc, aps)
    r = run(nc, [{"in_" + k: v for k, v in arrays.items()}], core_ids=[0]).results[0]
    y, rec = r["out_y"], r["out_rec"]

    def rows(lo, hi):
        return rec[:, :, lo:hi].transpose(2, 1, 0).reshape(hi - lo, LRU)
    xs, hs, xlast, hlast = rows(O_XS, O_HS), rows(O_HS, O_XL), rows(O_XL, O_HL), rows(O_HL, O_N)
    s_conv = np.concatenate([r["out_s_c"], xs[:, None]], 1)[None]
    win = (1, 1, WINDOW, N_KV, HEAD_DIM)
    swin = (1, NDEC, WINDOW, N_KV, HEAD_DIM)
    return (y[:SEQ].reshape(1, SEQ, D_MODEL), y[SEQ:].reshape(NDEC, 1, D_MODEL), r["out_p_k"].reshape(win),
            r["out_p_v"].reshape(win), xlast.reshape(1, 1, 3, LRU), hlast.reshape(1, 1, LRU),
            r["out_s_k"].reshape(swin), r["out_s_v"].reshape(swin), s_conv, hs.reshape(1, NDEC, LRU))
```
